# Optimizing a Trainium2 kernel written in Bass

```python
import jax, jax.numpy as jnp
from jax import lax
import numpy as np

D_MODEL = 1024
BATCH = 1
SEQ = 256
DEPTH = 1

A_HEAD_DIM = 64
A_HEADS = D_MODEL // A_HEAD_DIM
A_GROUP_SIZE = 4
A_KV_HEADS = A_HEADS // A_GROUP_SIZE
A_WIDTH = A_HEADS * A_HEAD_DIM
A_KV_WIDTH = A_KV_HEADS * A_HEAD_DIM
CMP_BLOCK = 32
CMP_STRIDE = 16
SEL_BLOCK = 64
N_SELECT = 16
WINDOW = 512
Q_BLOCK = 128
FORCE_SCORE = 1.0e4
POOL_WINDOWS = (2, 4, 8, 16)
B_WIDTH = D_MODEL
POOL_GROUP = B_WIDTH // len(POOL_WINDOWS)
HG_EXPAND = 128
C_WIDTH = D_MODEL
HG_HEADS = C_WIDTH // HG_EXPAND
HG_VDIM = C_WIDTH // HG_HEADS
HG_CHUNK = 64
N_BRANCH = 3
BRANCH_WIDTH = D_MODEL
NORM_EPS = 1e-6

SPLIT_SIZES = (
    A_WIDTH,
    A_KV_WIDTH, A_KV_WIDTH,
    A_KV_WIDTH, A_KV_WIDTH,
    A_KV_WIDTH, A_KV_WIDTH,
    3 * A_HEADS,
    A_WIDTH,
    B_WIDTH, B_WIDTH,
    C_WIDTH, C_WIDTH, C_WIDTH, C_WIDTH,
    N_BRANCH * D_MODEL,
)
SPLIT_POINTS = tuple(int(v) for v in np.cumsum(SPLIT_SIZES)[:-1])
N_IN = int(sum(SPLIT_SIZES))

kernel_name = 'hybrid_nsa_pool_hgrn2_block'

def rms_norm(x, gain):
    xf = x.astype(jnp.float32)
    y = xf * lax.rsqrt(jnp.mean(xf * xf, axis=-1, keepdims=True) + NORM_EPS)
    return (y * gain.astype(jnp.float32)).astype(x.dtype)

def masked_softmax(s, mask):
    s = jnp.where(mask, s.astype(jnp.float32), -jnp.inf)
    m = jnp.max(s, axis=-1, keepdims=True)
    m = jnp.where(jnp.isfinite(m), m, 0.0)
    p = jnp.exp(s - m)
    return p / jnp.maximum(jnp.sum(p, axis=-1, keepdims=True), 1e-30)

def nsa_mixer(q, kc, vc, ks, vs, kw, vw, gate_logits, pe_k, pe_v, w_ck, w_cv):
    B, T, G, HPG, DH = q.shape
    scale = DH ** -0.5
    n_c = (T - CMP_BLOCK) // CMP_STRIDE + 1
    c_start = jnp.arange(n_c) * CMP_STRIDE
    cidx = c_start[:, None] + jnp.arange(CMP_BLOCK)[None, :]
    ck = jnp.einsum('bcpgd,pde->bcge', kc[:, cidx] + pe_k[:, None, :], w_ck)
    cv = jnp.einsum('bcpgd,pde->bcge', vc[:, cidx] + pe_v[:, None, :], w_cv)
    c_end = c_start + CMP_BLOCK - 1
    n_s = T // SEL_BLOCK
    n_sel = min(N_SELECT, n_s)
    s_start = jnp.arange(n_s) * SEL_BLOCK
    overlap = jnp.clip(jnp.minimum(c_start[:, None] + CMP_BLOCK, s_start[None, :] + SEL_BLOCK)
                       - jnp.maximum(c_start[:, None], s_start[None, :]), 0).astype(jnp.float32) / CMP_BLOCK
    ksb = ks.reshape(B, n_s, SEL_BLOCK, G, DH).transpose(0, 3, 1, 2, 4)
    vsb = vs.reshape(B, n_s, SEL_BLOCK, G, DH).transpose(0, 3, 1, 2, 4)
    b_idx = jnp.arange(B)[:, None, None, None]
    g_idx = jnp.arange(G)[None, :, None, None]
    blk = jnp.arange(n_s)
    kw_pad = jnp.pad(kw, ((0, 0), (WINDOW, 0), (0, 0), (0, 0)))
    vw_pad = jnp.pad(vw, ((0, 0), (WINDOW, 0), (0, 0), (0, 0)))

    def block(i):
        s0 = i * Q_BLOCK
        t = s0 + jnp.arange(Q_BLOCK)
        qb = lax.dynamic_slice_in_dim(q, s0, Q_BLOCK, axis=1)
        gb = jax.nn.sigmoid(lax.dynamic_slice_in_dim(gate_logits, s0, Q_BLOCK, axis=1).astype(jnp.float32))
        sc = jnp.einsum('bqghd,bcgd->bghqc', qb, ck) * scale
        pc = masked_softmax(sc, c_end[None, :] <= t[:, None])
        oc = jnp.einsum('bghqc,bcgd->bqghd', pc, cv)
        imp = jnp.einsum('bghqc,cj->bgqj', pc, overlap)
        cur = t // SEL_BLOCK
        valid = blk[None, :] <= cur[:, None]
        force = (blk[None, :] == 0) | (blk[None, :] == cur[:, None]) | (blk[None, :] == cur[:, None] - 1)
        score = jnp.where(valid, jnp.where(force, FORCE_SCORE, imp), -1.0)
        _, idx = lax.top_k(score, n_sel)
        kg = ksb[b_idx, g_idx, idx]
        vg = vsb[b_idx, g_idx, idx]
        pos = idx[..., None] * SEL_BLOCK + jnp.arange(SEL_BLOCK)
        ss = jnp.einsum('bqghd,bgqnkd->bghqnk', qb, kg) * scale
        ms = (pos <= t[None, None, :, None, None]).reshape(B, G, 1, Q_BLOCK, n_sel * SEL_BLOCK)
        ps = masked_softmax(ss.reshape(B, G, HPG, Q_BLOCK, n_sel * SEL_BLOCK), ms)
        o_sel = jnp.einsum('bghqm,bgqmd->bqghd', ps, vg.reshape(B, G, Q_BLOCK, n_sel * SEL_BLOCK, DH))
        kwb = lax.dynamic_slice_in_dim(kw_pad, s0, Q_BLOCK + WINDOW, axis=1)
        vwb = lax.dynamic_slice_in_dim(vw_pad, s0, Q_BLOCK + WINDOW, axis=1)
        p = s0 - WINDOW + jnp.arange(Q_BLOCK + WINDOW)
        diff = t[:, None] - p[None, :]
        mw = (diff >= 0) & (diff < WINDOW) & (p[None, :] >= 0)
        sw = jnp.einsum('bqghd,bkgd->bghqk', qb, kwb) * scale
        pw = masked_softmax(sw, mw)
        ow = jnp.einsum('bghqk,bkgd->bqghd', pw, vwb)
        return gb[..., 0:1] * oc + gb[..., 1:2] * o_sel + gb[..., 2:3] * ow

    out = lax.map(block, jnp.arange(T // Q_BLOCK))
    return out.transpose(1, 0, 2, 3, 4, 5).reshape(B, T, G * HPG * DH).astype(q.dtype)

def pool_mixer(v, w_pool, scale):
    B, T, _ = v.shape
    vf = v.astype(jnp.float32)
    c = jnp.cumsum(vf, axis=1)
    count = jnp.arange(1, T + 1).astype(jnp.float32)[None, :, None]
    outs = []
    for g, w in enumerate(POOL_WINDOWS):
        sl = slice(g * POOL_GROUP, (g + 1) * POOL_GROUP)
        cg = c[..., sl]
        lo = jnp.pad(cg, ((0, 0), (w, 0), (0, 0)))[:, :T]
        outs.append((cg - lo) / jnp.minimum(count, float(w)) - vf[..., sl])
    pooled = jnp.stack(outs, axis=2)
    mixed = jnp.einsum('btgc,gcd->btgd', pooled, w_pool.astype(jnp.float32)).reshape(B, T, B_WIDTH)
    return (mixed * scale.astype(jnp.float32)).astype(v.dtype)

def hgrn2_mixer(q, f_logits, inp, lb):
    B, T, _ = q.shape
    H, DK, DV, C = HG_HEADS, HG_EXPAND, HG_VDIM, HG_CHUNK
    NC = T // C
    lb = lb.reshape(H, DK)
    f = lb + (1.0 - lb) * jax.nn.sigmoid(f_logits.astype(jnp.float32).reshape(B, T, H, DK))
    logf = jnp.log(f)
    k = 1.0 - f

    def chunks(a, d):
        return a.astype(jnp.float32).reshape(B, NC, C, H, d).transpose(1, 0, 3, 2, 4)

    qc, kc, lfc = chunks(q, DK), chunks(k, DK), chunks(logf, DK)
    vc = chunks(inp, DV)
    tri = jnp.tril(jnp.ones((C, C), dtype=bool))

    def step(S, xs):
        qq, kk, lf, vv = xs
        A = jnp.cumsum(lf, axis=2)
        o_inter = jnp.einsum('bhtd,bhde->bhte', qq * jnp.exp(A), S)
        rel = jnp.where(tri[:, :, None], A[:, :, :, None, :] - A[:, :, None, :, :], -jnp.inf)
        att = jnp.einsum('bhtd,bhsd,bhtsd->bhts', qq, kk, jnp.exp(rel))
        o_intra = jnp.einsum('bhts,bhse->bhte', att, vv)
        A_last = A[:, :, -1:, :]
        S = jnp.exp(A_last[:, :, 0, :])[..., None] * S + jnp.einsum('bhsd,bhse->bhde', kk * jnp.exp(A_last - A), vv)
        return S, o_inter + o_intra

    S0 = jnp.zeros((B, H, DK, DV), jnp.float32)
    _, o = lax.scan(step, S0, (qc, kc, lfc, vc))
    return o.transpose(1, 0, 3, 2, 4).reshape(B, T, H, DV).astype(q.dtype)

def setup_inputs(seed: int = 0) -> dict:
    key = jax.random.key(seed)
    ks = jax.random.split(key, 14)

    def nrm(k, shape, s):
        return jax.random.normal(k, shape, jnp.float32) * s

    return {
        'x': nrm(ks[0], (BATCH, SEQ, D_MODEL), 1.0),
        'pre_norm': 1.0 + nrm(ks[1], (DEPTH, D_MODEL), 0.05),
        'w_in': nrm(ks[2], (DEPTH, D_MODEL, N_IN), D_MODEL ** -0.5),
        'cmp_pe_k': nrm(ks[3], (DEPTH, CMP_BLOCK, A_HEAD_DIM), 0.1),
        'cmp_pe_v': nrm(ks[4], (DEPTH, CMP_BLOCK, A_HEAD_DIM), 0.1),
        'cmp_w_k': nrm(ks[5], (DEPTH, CMP_BLOCK, A_HEAD_DIM, A_HEAD_DIM), (CMP_BLOCK * A_HEAD_DIM) ** -0.5),
        'cmp_w_v': nrm(ks[6], (DEPTH, CMP_BLOCK, A_HEAD_DIM, A_HEAD_DIM), (CMP_BLOCK * A_HEAD_DIM) ** -0.5),
        'pool_w': nrm(ks[7], (DEPTH, len(POOL_WINDOWS), POOL_GROUP, POOL_GROUP), POOL_GROUP ** -0.5),
        'pool_scale': 1.0 + nrm(ks[8], (DEPTH, B_WIDTH), 0.1),
        'hgrn_lb_logits': nrm(ks[9], (DEPTH, C_WIDTH), 1.0),
        'hgrn_norm': 1.0 + nrm(ks[10], (DEPTH, C_WIDTH), 0.05),
        'w_branch': nrm(ks[11], (DEPTH, N_BRANCH, BRANCH_WIDTH, D_MODEL), BRANCH_WIDTH ** -0.5),
        'w_out': nrm(ks[12], (DEPTH, D_MODEL, D_MODEL), D_MODEL ** -0.5),
        'post_norm': 1.0 + nrm(ks[13], (DEPTH, D_MODEL), 0.05),
    }

def reference(x, pre_norm, w_in, cmp_pe_k, cmp_pe_v, cmp_w_k, cmp_w_v, pool_w, pool_scale,
              hgrn_lb_logits, hgrn_norm, w_branch, w_out, post_norm):
    B, T, _ = x.shape
    probs = jax.nn.softmax(hgrn_lb_logits.astype(jnp.float32), axis=0)
    lbs = jnp.cumsum(probs, axis=0) - probs[0]

    def kv(a):
        return a.reshape(B, T, A_KV_HEADS, A_HEAD_DIM)

    for l in range(DEPTH):
        h = rms_norm(x, pre_norm[l])
        z = jnp.einsum('btd,dn->btn', h, w_in[l])
        (a_q, a_kc, a_vc, a_ks, a_vs, a_kw, a_vw, a_gate, a_silu,
         b_v, b_silu, c_q, c_f, c_i, c_silu, merge_logits) = jnp.split(z, SPLIT_POINTS, axis=-1)
        o_a = nsa_mixer(a_q.reshape(B, T, A_KV_HEADS, A_GROUP_SIZE, A_HEAD_DIM),
                        kv(a_kc), kv(a_vc), kv(a_ks), kv(a_vs), kv(a_kw), kv(a_vw),
                        a_gate.reshape(B, T, A_KV_HEADS, A_GROUP_SIZE, 3),
                        cmp_pe_k[l], cmp_pe_v[l], cmp_w_k[l], cmp_w_v[l])
        o_a = o_a * jax.nn.silu(a_silu)
        o_b = pool_mixer(b_v, pool_w[l], pool_scale[l]) * jax.nn.silu(b_silu)
        o_c = hgrn2_mixer(c_q, c_f, c_i, lbs[l])
        o_c = rms_norm(o_c, hgrn_norm[l].reshape(HG_HEADS, HG_VDIM)).reshape(B, T, C_WIDTH) * jax.nn.silu(c_silu)
        branches = jnp.stack([o_a, o_b, o_c], axis=2)
        y = jnp.einsum('btnc,ncd->btnd', branches, w_branch[l])
        gates = jax.nn.sigmoid(merge_logits.reshape(B, T, N_BRANCH, D_MODEL))
        merged = jnp.sum(gates * y, axis=2)
        out = jnp.einsum('btd,de->bte', merged, w_out[l])
        x = x + rms_norm(out, post_norm[l])
    return x


_drawn_inputs = setup_inputs


def setup_inputs(seed=0):
    import zlib

    import numpy as np

    out = dict(_drawn_inputs(seed))
    spreads = {}
    factors = {}
    for name, (base, spread) in spreads.items():
        noise = np.random.default_rng([zlib.crc32(name.encode()), seed]).standard_normal(out[name].shape)
        drawn = base * np.exp(spread * noise) if base else spread * noise
        out[name] = __import__('jax').numpy.asarray(drawn.astype(out[name].dtype))
    for name, factor in factors.items():
        out[name] = (out[name] * factor).astype(out[name].dtype)
    return out
```

```python
from contextlib import ExitStack

import concourse.bass as bass
from concourse import mybir

F32 = mybir.dt.float32
F32R = mybir.dt.float32r
BF16 = mybir.dt.bfloat16
ALU = mybir.AluOpType
ACT = mybir.ActivationFunctionType
AX_X = mybir.AxisListType.X

P = 128
D = 1024
T = 256
KC = D // P
TT = T // P
SLAB = 256
HEADS, HEAD, GROUPS = 16, 64, 4
HPG = HEADS // GROUPS
CB, CS = 32, 16
NCMP = (T - CB) // CS + 1
SCALE = HEAD ** -0.5
HG = 8
EPS = 1e-6
WINDOWS = (2, 4, 8, 16)
LEVELS = (128, 64, 32, 16, 8, 4, 2, 1)

C_Q, C_KC, C_VC, C_KS, C_VS, C_KW, C_VW = 0, 1024, 1280, 1536, 1792, 2048, 2304
C_GATE, C_ASILU, C_BV, C_BSILU = 2560, 2608, 3632, 4656
C_HQ, C_HF, C_HI, C_CSILU, C_MERGE = 5680, 6704, 7728, 8752, 9776
GATES = 3 * HEADS

K_MASK, K_ID, K_ONE = 0, 448, 576
K_CMASK, K_VALID, K_COUNT = 704, 734, 736
K_ROWS, K_SEL, K_ALL = 800, 804, 1060
K_CAUSAL = K_ALL
V_PRE, V_LB, V_HN, V_PS, V_PEK, V_PEV = 0, 8, 16, 24, 32, 64
V_ALL = 96


def plan_slabs():
    out = [("f", n, "in", C_HF + n * SLAB) for n in range(4)]
    for n in range(4):
        out += [("hq", n, "in", C_HQ + n * SLAB), ("hv", n, "in", C_HI + n * SLAB)]
    out += [("kc", 0, "in", C_KC), ("vc", 0, "in", C_VC), ("ks", 0, "in", C_KS), ("kw", 0, "in", C_KW),
            ("vs", 0, "in", C_VS), ("vw", 0, "in", C_VW), ("gate", 0, "in", C_GATE)]
    out += [("bv", n, "in", C_BV + n * SLAB) for n in range(2)]
    out += [("q", n, "in", C_Q + n * SLAB) for n in range(4)]
    out += [("bv", n, "in", C_BV + n * SLAB) for n in range(2, 4)]
    for b, silu in ((2, C_CSILU), (1, C_BSILU), (0, C_ASILU)):
        out += [("silu", n, "in", silu + n * SLAB, b) for n in range(4)]
        for n in range(4):
            out += [("merge", n, "in", C_MERGE + b * D + n * SLAB, b), ("branch", n, b, n * SLAB, b)]
    out += [("out", n, "out", n * SLAB) for n in range(4)]
    return out


SLABS = plan_slabs()
NS = len(SLABS)
LAST = NS - 5
WHERE = {(s[0], s[1]) + tuple(s[4:]): i for i, s in enumerate(SLABS)}
TOKEN_MAJOR = ("hv", "vs", "vw", "gate", "out")
BY_ACT = ("f", "bv", "silu", "merge", "out")
BY_DVE = ("hq", "hv", "kc", "vc", "ks", "kw", "vs", "vw", "gate", "q", "silu", "branch", "out")
ACT_READS = [sum(x[0] in BY_ACT for x in SLABS[:i + 1]) for i in range(NS)]
DVE_READS = [sum(x[0] in BY_DVE for x in SLABS[:i + 1]) for i in range(NS)]

U0 = 9
CK, CV, CX, SC, TURN = 27, 28, 29, 30, 32
H0 = 30
G0 = 33
NU = HG * TT


def trunk(nc, x, small, consts, w_in, cmp_w, pool_w, w_branch, w_out, post_norm, out):
    ctx = ExitStack()
    with ctx:
        def sb(name, shape, dt=F32):
            return ctx.enter_context(nc.sbuf_tensor(name, shape, dt))

        def sem(name):
            return ctx.enter_context(nc.semaphore(name))

        ps = ctx.enter_context(nc.psum_tensor("ps", [P, 8, 512], F32))
        ps_flat = ps[:].rearrange("p a b -> p (a b)")

        W = sb("W", [P, 3, KC, SLAB])
        WH = sb("WH", [P, 3, KC, SLAB], F32R)
        WL = sb("WL", [P, 2, KC, SLAB], F32R)
        hH = sb("hH", [P, KC, T], F32R)
        hL = sb("hL", [P, KC, T], F32R)
        bH = sb("bH", [P, KC, T], F32R)
        bL = sb("bL", [P, KC, T], F32R)
        R = sb("R", [P, 8, 2048])
        OC = sb("OC", [P, HG, T])
        PM = sb("PM", [P, 2, 640])
        CP = sb("CP", [P, 2048])
        KD = sb("KD", [P, 2, GROUPS, T])
        VV = sb("VV", [P, 2, TT, SLAB])
        CVD = sb("CVD", [P, 4, GROUPS * HEAD])
        CKD = sb("CKD", [P, GROUPS, 2, 16])
        TG = sb("TG", [P, 2, 512])
        K = sb("K", [P, K_ALL])
        V = sb("V", [P, V_ALL])
        IB = sb("IB", [P, P], BF16)
        MB = sb("MB", [P, P], BF16)
        GT = sb("GT", [P, TT, GATES])
        st = sb("st", [P, 176])

        HK = R[:, 0, :].rearrange("p (h t) -> p h t", h=HG)
        HA = R[:, 1, :].rearrange("p (h t) -> p h t", h=HG)
        HQ = R[:, 2, :].rearrange("p (h t) -> p h t", h=HG)
        HV = R[:, 3, :].rearrange("p (i n) -> p i n", i=TT)
        QK = [R[:, 4 + 2 * b:6 + 2 * b, :].rearrange("p a (l h t) -> p (a l) h t", h=2, t=T) for b in range(2)]
        xin = R[:, 4, :].rearrange("p (i n) -> p i n", i=TT)
        sq = R[:, 5, :].rearrange("p (i n) -> p i n", i=TT)
        causal = R[:, 6, 0:P]
        qT = HK
        BV = HA
        PP = R[:, 2, 0:1536].rearrange("p (a n) -> p a n", a=2)
        M = R[:, 3, :].rearrange("p (c t) -> p c t", c=KC)
        WC = [R[:, 4 + 2 * b:6 + 2 * b, :].rearrange("p a (k n) -> p (a k) n", n=P) for b in range(2)]
        OA = R[:, 4, :].rearrange("p (c t) -> p c t", c=KC)
        PW = R[:, 5, :].rearrange("p (g k n) -> p g k n", g=4, k=2)
        MX = R[:, 6, :].rearrange("p (c t) -> p c t", c=KC)
        WA = R[:, 3, 1024:1536].rearrange("p (c t) -> p c t", c=2)
        WB = R[:, 3, 1536:2048].rearrange("p (c t) -> p c t", c=2)
        BR = R[:, 7, 1024:2048].rearrange("p (a n) -> p a n", a=2)
        BR2 = R[:, 3, 0:1024].rearrange("p (a n) -> p a n", a=2)
        XR = R[:, 0, :].rearrange("p (i n) -> p i n", i=TT)
        POST = R[:, 1, 0:D]
        Y = R[:, 4, :].rearrange("p (i n) -> p i n", i=TT)
        OUT = R[:, 6, :].rearrange("p (i n) -> p i n", i=TT)
        SQ = TG[:, 0, 0:T]
        LR = TG[:, 0, T:2 * T]
        RS = TG[:, 1, 0:T]
        PTS = PM[:].rearrange("p a b -> p (a b)")[:, 0:768]
        U = PM[:].rearrange("p a b -> p (a b)")[:, 768:1280]
        cpe = CP[:, 0:1920].rearrange("p (v k g c) -> p v k g c", v=2, k=CB, g=2)
        CSB = R[:, 2, 1536:1792].rearrange("p (a n) -> p a n", a=2)
        SM = CP[:, 1024:1504].rearrange("p (i h c) -> p i h c", i=TT, h=HEADS)
        PC = CP[:, 0:1024].rearrange("p (i h c) -> p i h c", i=TT, h=HEADS)
        PCT = CP[:, 1024:2048].rearrange("p (g t) -> p g t", g=GROUPS)
        ident = K[:, K_ID:K_ID + P]
        ones = K[:, K_ONE:K_ONE + P]
        st_x, st_r = st[:, 0:2], st[:, 2:4]
        st_lb = st[:, 8:48].rearrange("p (a h) -> p a h", a=5)
        st_hn, st_ps = st[:, 48:56], st[:, 56:64]
        st_eps = st[:, 64:65]
        st_nb = st[:, 66:74].rearrange("p (a n) -> p a n", a=2)
        st_sum = st[:, 74:82].rearrange("p (a n) -> p a n", a=2)
        st_w = st[:, 82:90].rearrange("p (a n) -> p a n", a=2)
        st_mx, st_cs = st[:, 90:122], st[:, 122:154]
        st_o = st[:, 154:162].rearrange("p (i n) -> p i n", i=TT)
        st_t, st_q = st[:, 162:164], st[:, 164:166]
        st_t4 = st[:, 166:170]

        s_small, s_x, s_xr, s_post = sem("small_in"), sem("x_in"), sem("xr_in"), sem("post_in")
        s_land = [sem(f"slab_in{i}") for i in range(3)]
        s_cw = [sem("cmp_wk_in"), sem("cmp_wv_in")]
        s_dup = [sem("ks_dup"), sem("kw_dup"), sem("ck_dup")]
        s_pw, s_out = sem("pool_w_in"), sem("out_done")
        s_xt, s_prod = sem("x_turned"), sem("slab_product")
        s_hp, s_hpv, s_hss = sem("hg_scores"), sem("hg_values"), sem("hg_squares")
        s_cpe = sem("cmp_pe")
        s_as, s_at, s_apv = sem("at_scores"), sem("at_turned"), sem("at_values")
        s_pmix = sem("pool_mixed")
        s_hi, s_read_a, s_bhi = sem("w_hi"), sem("act_read"), sem("branch_hi")
        s_hx, s_ac = sem("x_hi"), sem("act_chain")
        s_ln, s_hexp, s_hsq, s_hrs = sem("hg_ln"), sem("hg_exp"), sem("hg_sq"), sem("hg_rstd")
        s_cexp, s_exp, s_apt, s_aoa = sem("cmp_exp"), sem("at_exp"), sem("at_pt_act"), sem("at_out")
        s_pct_a, s_gt = sem("pct_act"), sem("gates_tanh")
        s_mhi, s_mfin = sem("merged_hi"), sem("merged_done")
        s_lo, s_read_v, s_blo, s_mlo = sem("w_lo"), sem("dve_read"), sem("branch_lo"), sem("merged_lo")
        s_dc, s_init, s_lx, s_xn = sem("dve_chain"), sem("dve_init"), sem("x_lo"), sem("x_normed")
        s_fk, s_scan, s_hmul, s_hmask = sem("f_done"), sem("hg_scan"), sem("hg_mul"), sem("hg_masked")
        s_hoc, s_hn = sem("hg_out"), sem("hg_normed")
        s_ckb, s_ck, s_cv, s_csm, s_cpc, s_pct = sem("ck_blocks"), sem("ck_out"), sem("cv_out"), sem("cmp_sm"), sem("cmp_probs"), sem("pct_dve")
        s_cvd, s_nb, s_aw, s_apv2 = sem("cvd_out"), sem("at_max"), sem("at_weight"), sem("at_pt_dve")
        s_br = sem("branch_out")
        s_px, s_gg = sem("pool_out"), sem("gates_done")
        s_fin, s_lbd, s_fin_ss = sem("final"), sem("lb_ready"), sem("out_squares")
        s_sub, s_scl, s_pool, s_zero, s_madd = (sem("hg_sub"), sem("at_scaled"), sem("pool_in"),
                                                sem("cmp_zero"), sem("merged_add"))
        s_pc = sem("pool_chain")

        def slab_source(s):
            kind, n, w, col = SLABS[s][:4]
            src = {"in": w_in[0], "out": w_out[0]}.get(w)
            if src is None:
                src = w_branch[0, w]
            width = GATES if kind == "gate" else SLAB
            return src[:, col:col + width].rearrange("(k p) n -> p k n", p=P), width

        def width(s):
            return GATES if SLABS[s][0] == "gate" else SLAB

        def bank(s):
            return ps[:, s % 2, :]

        def head(h):
            return h // 2, h % 2, h // HPG

        block = ctx.enter_context(nc.Block())

        @block.sync
        def _(sp):
            def load_slab(s):
                if s >= 3:
                    sp.wait_ge(s_lo, s - 2)
                src, n = slab_source(s)
                sp.dma_start(W[:, s % 3, :, 0:n], src).then_inc(s_land[s % 3], 16)

            sp.dma_start(xin, x[0].rearrange("(i p) n -> p i n", p=P)).then_inc(s_x, 16)
            sp.dma_start(V[:], small).then_inc(s_small, 16)
            sp.dma_start(K[:], consts[:, 0:K_ALL]).then_inc(s_small, 16)
            sp.dma_start(causal, consts[:, K_CAUSAL:K_CAUSAL + P]).then_inc(s_small, 16)
            for s in range(3):
                load_slab(s)
            for s in range(NS):
                if s + 3 < NS:
                    load_slab(s + 3)
                for a, kind in enumerate(("ks", "kw")):
                    if s == WHERE[(kind, 0)] + 3:
                        sp.wait_ge(s_read_v, DVE_READS[WHERE[(kind, 0)]])
                        kd = KD[:, a].rearrange("p (c g) t -> p c g t", g=2)
                        sp.dma_start(kd[64:128, :, 0], kd[0:64, :, 0]).then_inc(s_dup[a], 16)
                        sp.dma_start(kd[0:64, :, 1], kd[64:128, :, 1]).then_inc(s_dup[a], 16)
                for a, at in ((0, U0 + 11 + 3), (1, U0 + 15 + 3)):
                    if s == at:
                        sp.wait_ge(s_hp, 12 + 4 * a)
                        for half in range(2):
                            sp.dma_start(WC[a][64 * half:64 * half + 64, :, 64 * half:64 * half + 64],
                                         cmp_w[a].rearrange("k d e -> d k e")).then_inc(s_cw[a], 16)
                if s == CK + 3:
                    sp.wait_ge(s_cpe, 1)
                    for g in range(4):
                        sp.dma_start(PW[:, g], pool_w[0, g].rearrange("(k p) n -> p k n", p=P)).then_inc(s_pw, 16)
                if s == NS - 8:
                    sp.wait_ge(s_as, HEADS)
                    sp.wait_ge(s_pool, 4)
                    sp.dma_start(XR, x[0].rearrange("(i p) n -> p i n", p=P)).then_inc(s_xr, 16)
                    sp.dma_start(POST, post_norm.to_broadcast((P, D))).then_inc(s_post, 16)
            for i in range(TT):
                sp.wait_ge(s_fin, i + 1)
                sp.dma_start(out[0, i * P:(i + 1) * P, :], OUT[:, i, :]).then_inc(s_out, 16)
            sp.wait_ge(s_out, 16 * TT)

        @block.gpsimd
        def _(pool):
            chain = [0]

            def link(ins):
                chain[0] += 1
                ins.then_inc(s_pc, 1)
                pool.wait_ge(s_pc, chain[0])

            for p in range(4):
                pool.wait_ge(s_scan, p + 1)
                if p >= 2:
                    pool.wait_ge(s_hp, 4 * (p - 1))
                else:
                    pool.wait_ge(s_xn, 2)
                    pool.wait_ge(s_xt, 4)
                a2 = HA[:, 2 * p:2 * p + 2, :].rearrange("p h t -> p (h t)")
                for i, b in enumerate(LEVELS):
                    n = 2 * T // (2 * b)
                    av = a2.rearrange("p (n w) -> p n w", w=2 * b)
                    dv = QK[p % 2][:, i].rearrange("p h t -> p (h t)").rearrange("p (n w) -> p n w", w=2 * b)
                    edge = av[:, :, b - 1:b].to_broadcast((P, n, b))
                    last = pool.tensor_tensor(dv[:, :, 0:b], edge, av[:, :, 0:b], ALU.subtract)
                    if i:
                        last = pool.tensor_tensor(dv[:, :, b:2 * b], av[:, :, b:2 * b], edge, ALU.subtract)
                last.then_inc(s_sub, 1)
            for a in range(2):
                pool.wait_ge(s_hp, 12 + 4 * a)
                pool.wait_ge(s_sub, 4)
                if a:
                    pool.wait_ge(s_zero, 2)
                pool.memset(WC[a][0:64, :, 64:128], 0.0).then_inc(s_zero, 1)
                pool.wait_ge(s_zero, 2 * a + 1)
                pool.memset(WC[a][64:128, :, 0:64], 0.0).then_inc(s_zero, 1)
            pool.wait_ge(s_zero, 4)
            pool.wait_ge(s_hpv, NU)

            def pool_group(g):
                w = WINDOWS[g]
                src = BV[:, 2 * g:2 * g + 2, :]
                if g == 0:
                    pool.wait_ge(s_read_a, ACT_READS[WHERE[("bv", 3)]])
                else:
                    pool.wait_ge(s_pool, g)
                cur, sh, flip = src, 1, 0
                while sh < w:
                    dst = (WA, WB)[flip]
                    link(pool.tensor_tensor(dst[:, :, sh:T], cur[:, :, sh:T], cur[:, :, 0:T - sh], ALU.add))
                    link(pool.tensor_copy(dst[:, :, 0:sh], cur[:, :, 0:sh]))
                    cur, sh, flip = dst, sh * 2, 1 - flip
                dst = (WA, WB)[flip]
                link(pool.tensor_scalar(dst, cur, 1.0 / w, None, ALU.mult))
                cnt = K[:, K_COUNT + 16 * g:K_COUNT + 16 * g + w].rearrange("p (a n) -> p a n", a=1)
                link(pool.tensor_tensor(dst[:, :, 0:w], cur[:, :, 0:w], cnt.to_broadcast((P, 2, w)), ALU.mult))
                pool.tensor_tensor(src, dst, src, ALU.subtract).then_inc(s_pool, 1)

            def scale_head(h):
                pool.wait_ge(s_aw, h + 1)
                w = st_w[:, h % 2]
                pp = PP[:, h % 2]
                for j in range(2):
                    pool.tensor_scalar(pp[:, 256 * j:256 * j + 256], pp[:, 256 * j:256 * j + 256],
                                       w[:, j:j + 1], None, ALU.mult)
                for j in range(2):
                    last = pool.tensor_scalar(pp[:, 512 + 128 * j:640 + 128 * j], pp[:, 512 + 128 * j:640 + 128 * j],
                                              w[:, 2 + j:3 + j], None, ALU.mult)
                last.then_inc(s_scl, 1)

            def add_merged(b, n):
                k = 4 * (2 - b) + n
                pool.wait_ge(s_read_v, DVE_READS[WHERE[("branch", n, b)]])
                m = M[:, 2 * n:2 * n + 2, :].rearrange("p c t -> p (c t)")
                if b < 2:
                    pool.wait_ge(s_madd, k - 3)
                    pool.tensor_tensor(m, m, U, ALU.add).then_inc(s_madd, 1)
                else:
                    pool.tensor_copy(m, U).then_inc(s_madd, 1)

            for g in range(4):
                pool_group(g)
            for s in range(H0, NS):
                if H0 <= s < H0 + HEADS:
                    scale_head(s - H0)
                if SLABS[s][0] == "branch" and SLABS[s][4]:
                    add_merged(SLABS[s][4], SLABS[s][1])

        @block.scalar
        def _(act):
            chain = [0]

            def link(ins):
                chain[0] += 1
                ins.then_inc(s_ac, 1)
                act.wait_ge(s_ac, chain[0])

            def hi(s):
                act.wait_ge(s_land[s % 3], 16 * (s // 3 + 1))
                if s >= 3:
                    act.wait_ge(s_prod, s - 2)
                n = width(s)
                act.activation(WH[:, s % 3, :, 0:n], W[:, s % 3, :, 0:n], ACT.Copy).then_inc(s_hi, 1)

            def mix(s):
                if s == U0 - 5:
                    for p in range(4):
                        act.wait_ge(s_fk, p + 1)
                        f = OC[:, 2 * p:2 * p + 2, :]
                        act.activation(f, f, ACT.Ln).then_inc(s_ln, 1)
                for p in range(4):
                    if s == U0 - 3 + 4 * p:
                        act.wait_ge(s_sub, p + 1)
                        act.wait_ge(s_scan, p + 1)
                        q = QK[p % 2]
                        act.activation(q[:, 0, :, P:T], HA[:, 2 * p:2 * p + 2, P:T], ACT.Exp)
                        act.activation(q[:, 0, :, 0:P], q[:, 0, :, 0:P], ACT.Exp)
                        act.activation(q[:, 1:8].rearrange("p l h t -> p (l h t)"),
                                       q[:, 1:8].rearrange("p l h t -> p (l h t)"), ACT.Exp).then_inc(s_hexp, 1)
                for h in range(HG):
                    if s == U0 + 2 + 2 * h:
                        act.wait_ge(s_hoc, h + 1)
                        act.activation(SQ, OC[:, h, :], ACT.Square).then_inc(s_hsq, 1)
                    if s == U0 + 3 + 2 * h:
                        act.wait_ge(s_hss, h + 1)
                        if h:
                            act.wait_ge(s_hn, h)
                        link(act.activation(LR, ps[:, 7, 0:T], ACT.Ln, scale=1.0 / P, bias=st_eps))
                        act.activation(RS, LR, ACT.Exp, scale=-0.5).then_inc(s_hrs, 1)
                if s == CK:
                    act.wait_ge(s_read_v, DVE_READS[WHERE[("gate", 0)]])
                    act.activation(GT[:], GT[:], ACT.Tanh, scale=0.5).then_inc(s_gt, 1)
                if s == CX:
                    act.wait_ge(s_ckb, 1)
                    kd = CKD[:].rearrange("p (c g) b n -> p c g b n", g=2)
                    act.dma_start(kd[64:128, :, 0, 1, 0:NCMP], kd[0:64, :, 0, 0, 0:NCMP]).then_inc(s_dup[2], 16)
                    act.dma_start(kd[0:64, :, 1, 0, 0:NCMP], kd[64:128, :, 1, 1, 0:NCMP]).then_inc(s_dup[2], 16)
                if s == SC:
                    act.wait_ge(s_csm, 1)
                    sm = SM.rearrange("p i h c -> p (i h c)")
                    act.activation(sm, sm, ACT.Exp).then_inc(s_cexp, 1)
                if s == TURN:
                    act.wait_ge(s_cpe, 6)
                    act.activation(PCT[:, 0:2].rearrange("p g t -> p (g t)"), ps[:, 6, :],
                                   ACT.Copy).then_inc(s_pct_a, 1)
                h = s - H0
                if 0 <= h < HEADS:
                    act.wait_ge(s_nb, h + 1)
                    if h >= 2:
                        act.wait_ge(s_at, h - 1)
                    pp, nb, sm = PP[:, h % 2], st_nb[:, h % 2], st_sum[:, h % 2]
                    for j in range(2):
                        act.activation(pp[:, 256 * j:256 * j + 256], ps[:, 2, 256 * j:256 * j + 256], ACT.Exp,
                                       bias=nb[:, j:j + 1], scale=SCALE, accum_out=sm[:, j:j + 1])
                    for j in range(2):
                        last = act.activation(pp[:, 512 + 128 * j:640 + 128 * j], ps[:, 3, 128 * j:128 * j + 128],
                                              ACT.Exp, bias=nb[:, 2 + j:3 + j], scale=SCALE,
                                              accum_out=sm[:, 2 + j:3 + j])
                    last.then_inc(s_exp, 1)
                h = s - H0 - 2
                if 0 <= h < HEADS:
                    act.wait_ge(s_at, h + 1)
                    if h:
                        act.wait_ge(s_apv, h)
                    act.activation(PTS[:, 0:512], ps[:, 4, :], ACT.Copy).then_inc(s_apt, 1)
                h = s - H0 - 3
                if 0 <= h < HEADS and h % 2:
                    act.wait_ge(s_apv, h + 1)
                    act.activation(OA[:, h // 2, :], ps[:, 6, 0:T], ACT.Copy, scale=0.5).then_inc(s_aoa, 1)
                if s >= 1 and SLABS[s - 1][0] == "silu":
                    n, b = SLABS[s - 1][1], SLABS[s - 1][4]
                    k = 4 * (2 - b) + n
                    act.wait_ge(s_br, k + 1)
                    if b < 2:
                        act.wait_ge(s_prod, WHERE[("branch", 3, b + 1)] + 1)
                    act.activation(bH[:, 2 * n:2 * n + 2, :].rearrange("p c t -> p (c t)"), (BR2 if k < 4 else BR)[:, k % 2, :],
                                   ACT.Copy).then_inc(s_bhi, 1)
                if s == LAST:
                    for n in range(3):
                        merged_hi(n)

            def merged_hi(n):
                act.wait_ge(s_mfin, n + 1)
                act.wait_ge(s_prod, WHERE[("merge", 3, 0)] + 1)
                act.activation(hH[:, 2 * n:2 * n + 2, :].rearrange("p c t -> p (c t)"),
                               M[:, 2 * n:2 * n + 2, :].rearrange("p c t -> p (c t)"),
                               ACT.Copy, scale=0.5).then_inc(s_mhi, 1)

            def read(s):
                kind, n = SLABS[s][:2]
                if kind not in BY_ACT:
                    return
                act.wait_ge(s_prod, s + 1)
                if kind == "f":
                    act.activation(OC[:, 2 * n:2 * n + 2, :].rearrange("p c t -> p (c t)"), bank(s),
                                   ACT.Sigmoid).then_inc(s_read_a, 1)
                elif kind == "bv":
                    act.wait_ge(s_sub, 4)
                    act.activation(BV[:, 2 * n:2 * n + 2, :].rearrange("p c t -> p (c t)"), bank(s),
                                   ACT.Copy).then_inc(s_read_a, 1)
                elif kind in ("silu", "merge"):
                    if s == WHERE[("silu", 0, 2)]:
                        act.wait_ge(s_hn, HG)
                    if s >= WHERE[("silu", 2, 2)]:
                        act.wait_ge(s_read_v, DVE_READS[s - 1] - (0 if SLABS[s - 1][0] == "branch" else 1))
                    act.activation(TG[:, tslot(s), :], bank(s), ACT.Tanh, scale=0.5).then_inc(s_read_a, 1)
                else:
                    if n:
                        act.wait_ge(s_read_a, ACT_READS[s - 1])
                    for i in range(TT):
                        last = act.activation(PP[:, i, 0:256], bank(s)[:, 256 * i:256 * i + 256], ACT.Square,
                                              accum_out=st_o[:, i, n:n + 1])
                    last.then_inc(s_read_a, 1)

            act.wait_ge(s_x, 16)
            act.activation(sq[:, 0, :], xin[:, 0, :], ACT.Square, accum_out=st_x[:, 0:1])
            act.activation(sq[:, 1, :], xin[:, 1, :], ACT.Square, accum_out=st_x[:, 1:2]).then_inc(s_hx, 1)
            act.wait_ge(s_hx, 1)
            act.wait_ge(s_init, 1)
            act.activation(st_t, st_x, ACT.Sqrt, scale=1.0 / D, bias=st_eps).then_inc(s_hx, 1)
            act.wait_ge(s_lbd, 1)
            act.activation(st_lb[:, 1], st_lb[:, 0], ACT.Exp).then_inc(s_hx, 1)
            hi(0)
            for c in range(KC):
                act.wait_ge(s_xt, c // 2 + 1)
                act.activation(hH[:, c, :], ps[:, 2 + c // 2, 256 * (c % 2):256 * (c % 2) + 256], ACT.Copy,
                               scale=V[:, V_PRE + c:V_PRE + c + 1]).then_inc(s_hx, 1)
            for s in range(1, 3):
                hi(s)
            for s in range(NS):
                mix(s)
                read(s)
                if s == LAST:
                    merged_hi(3)
                if s + 3 < NS:
                    hi(s + 3)
            act.wait_ge(s_fin_ss, 1)
            act.activation(st_q, st_t, ACT.Sqrt, scale=1.0 / D, bias=st_eps).then_inc(s_hx, 1)

        @block.vector
        def _(dve):
            chain = [0]

            def link(ins):
                chain[0] += 1
                ins.then_inc(s_dc, 1)
                dve.wait_ge(s_dc, chain[0])

            def lo(s):
                dve.wait_ge(s_hi, s + 1)
                if s >= 2:
                    dve.wait_ge(s_prod, s - 1)
                n = width(s)
                dve.tensor_tensor(WL[:, s % 2, :, 0:n], W[:, s % 3, :, 0:n], WH[:, s % 3, :, 0:n],
                                  ALU.subtract).then_inc(s_lo, 1)

            def forget(p):
                dve.wait_ge(s_read_a, ACT_READS[WHERE[("f", p)]])
                for h in range(2 * p, 2 * p + 2):
                    last = dve.tensor_scalar(OC[:, h, :], OC[:, h, :], st_lb[:, 4, h:h + 1], st_lb[:, 3, h:h + 1],
                                             ALU.mult, ALU.add)
                link(last)
                link(dve.tensor_scalar(HK[:, 2 * p:2 * p + 2, :], OC[:, 2 * p:2 * p + 2, :], -1.0, 1.0,
                                       ALU.mult, ALU.add))
                dve.tensor_scalar(OC[:, 2 * p:2 * p + 2, :], OC[:, 2 * p:2 * p + 2, :], 1e-18, None,
                                  ALU.max).then_inc(s_fk, 1)

            def mix(s):
                if 1 <= s <= 4:
                    forget(s - 1)
                if s in (4, 5, 6, 7):
                    p = s - 4
                    dve.wait_ge(s_ln, p + 1)
                    for h in range(2 * p, 2 * p + 2):
                        for i in range(TT):
                            last = dve.tensor_tensor_scan(HA[:, h, i * P:(i + 1) * P], ones,
                                                          OC[:, h, i * P:(i + 1) * P], 0.0, ALU.mult, ALU.add)
                    last.then_inc(s_scan, 1)
                u = s - U0
                if 0 <= u < NU:
                    dve.wait_ge(s_hp, u + 1)
                    if u >= 2:
                        dve.wait_ge(s_hpv, u - 1)
                    b0 = 2 + 2 * (u % 2)
                    n = P * (1 + u % 2)
                    link(dve.tensor_tensor(PM[:, u % 2, 0:n], ps[:, b0 + 1, 0:n], K[:, K_ID:K_ID + n], ALU.mult))
                    for lv in range(1, 8):
                        b = LEVELS[lv]
                        to = PM[:, u % 2, 0:P].rearrange("p (n w) -> p n w", w=2 * b)[:, :, b:2 * b]
                        c = slice(64 * (lv - 1), 64 * lv)
                        last = dve.copy_predicated(to, K[:, c].bitcast(mybir.dt.uint32).rearrange(
                            "p (n w) -> p n w", w=b), ps[:, b0, c].rearrange("p (n w) -> p n w", w=b))
                        if lv < 7:
                            link(last)
                    last.then_inc(s_hmask, 1)
                for h in range(HG):
                    if s == U0 + 2 + 2 * h:
                        dve.wait_ge(s_hpv, 2 * h + 2)
                        dve.tensor_copy(OC[:, h, :], ps[:, 6, 0:T]).then_inc(s_hoc, 1)
                    if s == U0 + 3 + 2 * h:
                        dve.wait_ge(s_hrs, h + 1)
                        dve.scalar_tensor_tensor(out=OC[:, h, :], in0=OC[:, h, :], scalar=st_hn[:, h:h + 1], in1=RS,
                                                 op0=ALU.mult, op1=ALU.mult).then_inc(s_hn, 1)
                for h in range(HG):
                    if s == U0 - 2 + 2 * h:
                        dve.wait_ge(s_hexp, h // 2 + 1)
                        for i, b in enumerate(LEVELS):
                            ev = QK[h // 2 % 2][:, i, h % 2].rearrange("p (n w) -> p n w", w=2 * b)
                            kv = HK[:, h].rearrange("p (n w) -> p n w", w=2 * b)
                            qv = HQ[:, h].rearrange("p (n w) -> p n w", w=2 * b)
                            dve.tensor_tensor(ev[:, :, 0:b], ev[:, :, 0:b], kv[:, :, 0:b], ALU.mult)
                            last = dve.tensor_tensor(ev[:, :, b:2 * b], ev[:, :, b:2 * b], qv[:, :, b:2 * b], ALU.mult)
                        link(last)
                        dve.tensor_tensor(HQ[:, h], HQ[:, h], HK[:, h], ALU.mult).then_inc(s_hmul, 1)
                if s == CK:
                    dve.wait_ge(s_cpe, 1)
                    dve.tensor_copy(CSB[0:2 * NCMP, 0, :], ps[0:2 * NCMP, 7, 0:P]).then_inc(s_ck, 1)
                    link(dve.memset(CKD[:], 0.0))
                if s == CV:
                    dve.wait_ge(s_cpe, 2)
                    ckd = CKD[:].rearrange("p (c g) b n -> p c g b n", g=2)
                    pk = ps[:, 6, 0:2 * NCMP].rearrange("p (g c) -> p g c", g=2)
                    dve.tensor_copy(ckd[0:64, :, 0, 0, 0:NCMP], pk[0:64])
                    dve.tensor_copy(ckd[64:128, :, 1, 1, 0:NCMP], pk[64:128]).then_inc(s_ckb, 1)
                    dve.wait_ge(s_cpe, 3)
                    dve.tensor_copy(CSB[0:2 * NCMP, 1, :], ps[0:2 * NCMP, 7, 0:P]).then_inc(s_cv, 1)
                if s == CX:
                    link(dve.memset(PC.rearrange("p i h c -> p (i h c)"), 0.0))
                    dve.wait_ge(s_gt, 1)
                    dve.tensor_scalar(GT[:], GT[:], 1.0, 0.5, ALU.add, ALU.mult).then_inc(s_gg, 1)
                    dve.wait_ge(s_cpe, 4)
                    for i in range(4):
                        last = dve.tensor_scalar(CVD[:, i, :], ps[:, 6, 0:256], K[:, K_ROWS + i:K_ROWS + i + 1], None,
                                                 ALU.mult)
                    last.then_inc(s_cvd, 1)
                if s == SC:
                    dve.wait_ge(s_cpe, 5)
                    for i in range(TT):
                        sc = ps[:, 7, 256 * i:256 * i + 256].rearrange("p (h c) -> p h c", c=16)
                        cm = K[:, K_CMASK + 15 * i:K_CMASK + 15 * i + 15].rearrange("p (a c) -> p a c", a=1)
                        last = dve.scalar_tensor_tensor(out=SM[:, i], in0=sc[:, :, 0:NCMP], scalar=SCALE,
                                                        in1=cm.to_broadcast((P, HEADS, NCMP)),
                                                        op0=ALU.mult, op1=ALU.add)
                    link(last)
                    smf = SM.rearrange("p i h c -> p (i h) c")
                    link(dve.tensor_reduce(st_mx, smf, AX_X, ALU.max))
                    mxv = st_mx.rearrange("p (h c) -> p h c", c=1)
                    dve.tensor_tensor(smf, smf, mxv.to_broadcast((P, 32, NCMP)), ALU.subtract).then_inc(s_csm, 1)
                if s == SC + 1:
                    dve.wait_ge(s_cexp, 1)
                    dve.wait_ge(s_gg, 1)
                    smf = SM.rearrange("p i h c -> p (i h) c")
                    link(dve.tensor_reduce(st_cs, smf, AX_X, ALU.add))
                    link(dve.tensor_scalar(st_cs, st_cs, 1e-30, None, ALU.max))
                    link(dve.reciprocal(st_cs, st_cs))
                    for i in range(TT):
                        gv = GT[:, i, :].rearrange("p (h j) -> p h j", j=3)[:, :, 0]
                        last = dve.scalar_tensor_tensor(out=st_mx[:, 16 * i:16 * i + 16],
                                                        in0=st_cs[:, 16 * i:16 * i + 16],
                                                        scalar=K[:, K_VALID + i:K_VALID + i + 1], in1=gv,
                                                        op0=ALU.mult, op1=ALU.mult)
                    link(last)
                    mxv = st_mx.rearrange("p (h c) -> p h c", c=1)
                    dve.tensor_tensor(PC.rearrange("p i h c -> p (i h) c")[:, :, 0:NCMP], smf,
                                      mxv.to_broadcast((P, 32, NCMP)), ALU.mult).then_inc(s_cpc, 1)
                if s == TURN:
                    dve.wait_ge(s_cpe, 6)
                    dve.tensor_copy(PCT[:, 2:4].rearrange("p g t -> p (g t)"), ps[:, 7, :]).then_inc(s_pct, 1)
                h = s - H0
                if 0 <= h < HEADS:
                    dve.wait_ge(s_as, h + 1)
                    dve.tensor_reduce(st_t4[:, 0:2], ps[:, 2, :].rearrange("p (a k) -> p a k", a=2), AX_X, ALU.max)
                    link(dve.tensor_reduce(st_t4[:, 2:4], ps[:, 3, 0:256].rearrange("p (a k) -> p a k", a=2),
                                           AX_X, ALU.max))
                    dve.tensor_scalar(st_nb[:, h % 2], st_t4, -SCALE, None, ALU.mult).then_inc(s_nb, 1)
                h = s - H0 - 2
                if 0 <= h < HEADS:
                    dve.wait_ge(s_at, h + 1)
                    if h:
                        dve.wait_ge(s_apv, h)
                    dve.tensor_copy(PTS[:, 512:768], ps[:, 5, 0:256]).then_inc(s_apv2, 1)
                g = s - G0
                if 0 <= g < 4:
                    dve.wait_ge(s_pmix, g + 1)
                    for c in range(2):
                        last = dve.tensor_scalar(MX[:, 2 * g + c, :], ps[:, 7, 256 * c:256 * c + 256],
                                                 st_ps[:, 2 * g + c:2 * g + c + 1], None, ALU.mult)
                    last.then_inc(s_px, 1)
                if s >= 1 and SLABS[s - 1][0] == "silu":
                    n, b = SLABS[s - 1][1], SLABS[s - 1][4]
                    k = 4 * (2 - b) + n
                    dve.wait_ge(s_bhi, k + 1)
                    dve.tensor_tensor(bL[:, 2 * n:2 * n + 2, :].rearrange("p c t -> p (c t)"), (BR2 if k < 4 else BR)[:, k % 2, :],
                                      bH[:, 2 * n:2 * n + 2, :].rearrange("p c t -> p (c t)"),
                                      ALU.subtract).then_inc(s_blo, 1)
                if s == LAST:
                    for n in range(3):
                        merged_lo(n)

            def merged_lo(n):
                dve.wait_ge(s_mhi, n + 1)
                dve.scalar_tensor_tensor(out=hL[:, 2 * n:2 * n + 2, :].rearrange("p c t -> p (c t)"),
                                         in0=M[:, 2 * n:2 * n + 2, :].rearrange("p c t -> p (c t)"), scalar=0.5,
                                         in1=hH[:, 2 * n:2 * n + 2, :].rearrange("p c t -> p (c t)"),
                                         op0=ALU.mult, op1=ALU.subtract).then_inc(s_mlo, 1)

            def late(s):
                h = s - H0
                if 0 <= h < HEADS:
                    dve.wait_ge(s_exp, h + 1)
                    if h >= 2:
                        dve.wait_ge(s_scl, h - 1)
                    w = st_w[:, h % 2]
                    link(dve.tensor_scalar(w, st_sum[:, h % 2], 1e-30, None, ALU.max))
                    link(dve.reciprocal(w, w))
                    dve.tensor_tensor(w[:, 0:2], w[:, 0:2], GT[:, 1, 3 * h + 1:3 * h + 3], ALU.mult)
                    dve.tensor_tensor(w[:, 2:4], w[:, 2:4], GT[:, 0, 3 * h + 1:3 * h + 3], ALU.mult)\
                        .then_inc(s_aw, 1)

            def read(s):
                kind, n = SLABS[s][:2]
                if kind not in BY_DVE:
                    return
                dve.wait_ge(s_prod, s + 1)
                if kind in ("silu", "branch", "out"):
                    dve.wait_ge(s_read_a, ACT_READS[s if kind != "branch" else s - 1])
                b = bank(s)
                b2 = b.rearrange("p (c t) -> p c t", c=2)
                if kind == "hq":
                    last = dve.tensor_copy(HQ[:, 2 * n:2 * n + 2, :], b2)
                elif kind == "q":
                    last = dve.tensor_copy(qT[:, 2 * n:2 * n + 2, :], b2)
                elif kind == "hv":
                    last = dve.tensor_copy(HV[:, :, SLAB * n:SLAB * n + SLAB], b2)
                elif kind in ("kc", "vc"):
                    v = 0 if kind == "kc" else 1
                    for g in range(2):
                        src = b[:, 256 * g:256 * g + 256]
                        pe = V[:, V_PEK + 32 * v:V_PEK + 32 * v + 32]
                        for half in range(2):
                            win = src[:, 16 * half:16 * half + 240].rearrange("p (c k) -> p k c", k=16)
                            ph = pe[:, 16 * half:16 * half + 16].rearrange("p (k c) -> p k c", c=1)
                            last = dve.tensor_tensor(cpe[:, v, 16 * half:16 * half + 16, g, :], win,
                                                     ph.to_broadcast((P, 16, NCMP)), ALU.add)
                elif kind in ("ks", "kw"):
                    kd = KD[:, 0 if kind == "ks" else 1].rearrange("p (c g) t -> p c g t", g=2)
                    dve.tensor_copy(kd[0:64, :, 0], b2[0:64])
                    last = dve.tensor_copy(kd[64:128, :, 1], b2[64:128])
                elif kind in ("vs", "vw"):
                    last = dve.tensor_copy(VV[:, 0 if kind == "vs" else 1], b2)
                elif kind == "gate":
                    last = dve.tensor_copy(GT[:], b[:, 0:TT * GATES].rearrange("p (i n) -> p i n", i=TT))
                elif kind == "silu":
                    br = SLABS[s][4]
                    k = 4 * (2 - br) + n
                    if br < 2 and n == 0:
                        dve.wait_ge(s_madd, 4 * (2 - br))
                    dve.scalar_tensor_tensor(out=U, in0=TG[:, tslot(s), :], scalar=1.0, in1=b, op0=ALU.add,
                                             op1=ALU.mult).then_inc(s_read_v, 1)
                    dve.wait_ge(s_read_v, DVE_READS[s])
                    src = (OA, MX, OC)[br][:, 2 * n:2 * n + 2, :].rearrange("p c t -> p (c t)")
                    if br == 0:
                        dve.wait_ge(s_aoa, HG)
                    if br == 1:
                        dve.wait_ge(s_px, 4)
                    if k >= 2:
                        dve.wait_ge(s_bhi, k - 1)
                    dve.tensor_tensor((BR2 if k < 4 else BR)[:, k % 2, :], src, U, ALU.mult).then_inc(s_br, 1)
                    return
                elif kind == "branch":
                    br = SLABS[s][4]
                    k = 4 * (2 - br) + n
                    if k:
                        dve.wait_ge(s_madd, min(k, 8))
                    if k > 8:
                        dve.wait_ge(s_mfin, k - 8)
                    dve.scalar_tensor_tensor(out=U, in0=TG[:, tslot(s - 1), :], scalar=1.0, in1=b, op0=ALU.add,
                                             op1=ALU.mult).then_inc(s_read_v, 1)
                    if br == 0:
                        dve.wait_ge(s_read_v, DVE_READS[s])
                        m = M[:, 2 * n:2 * n + 2, :].rearrange("p c t -> p (c t)")
                        dve.tensor_tensor(m, m, U, ALU.add).then_inc(s_mfin, 1)
                    return
                elif kind == "out":
                    dve.wait_ge(s_post, 16)
                    pv = POST[:, SLAB * n:SLAB * n + SLAB].rearrange("p (a n) -> p a n", a=1)
                    last = dve.tensor_tensor(Y[:, :, SLAB * n:SLAB * n + SLAB], b2,
                                             pv.to_broadcast((P, TT, SLAB)), ALU.mult)
                last.then_inc(s_read_v, 1)

            dve.memset(st_eps, EPS).then_inc(s_init, 1)
            dve.wait_ge(s_small, 48)
            dve.tensor_tensor(st_lb[:, 0], V[:, V_LB:V_LB + 8], V[:, V_LB:V_LB + 8], ALU.subtract).then_inc(s_lbd, 1)
            dve.tensor_copy(IB[:], ident)
            dve.tensor_copy(MB[:], causal)
            dve.tensor_copy(st_hn, V[:, V_HN:V_HN + 8])
            link(dve.tensor_scalar(st_ps, V[:, V_PS:V_PS + 8], 0.5, None, ALU.mult))
            link(dve.tensor_scalar(st_hn, st_hn, 0.5, None, ALU.mult))
            dve.wait_ge(s_hx, 2)
            link(dve.reciprocal(st_r, st_t))
            for i in range(TT):
                dve.tensor_scalar(xin[:, i, :], xin[:, i, :], st_r[:, i:i + 1], None, ALU.mult).then_inc(s_xn, 1)
            dve.wait_ge(s_hx, 3)
            link(dve.reciprocal(st_lb[:, 2], st_lb[:, 1]))
            link(dve.tensor_tensor(st_lb[:, 2], st_lb[:, 2], st_lb[:, 1], ALU.mult))
            link(dve.tensor_tensor(st_lb[:, 3], st_lb[:, 2], st_lb[:, 2], ALU.subtract))
            link(dve.tensor_scalar(st_lb[:, 4], st_lb[:, 3], -1.0, 1.0, ALU.mult, ALU.add))
            lo(0)
            for c in range(KC):
                dve.wait_ge(s_hx, 3 + 2 * (c // 2) + 2)
                dve.scalar_tensor_tensor(out=hL[:, c, :], in0=ps[:, 2 + c // 2, 256 * (c % 2):256 * (c % 2) + 256],
                                         scalar=V[:, V_PRE + c:V_PRE + c + 1], in1=hH[:, c, :],
                                         op0=ALU.mult, op1=ALU.subtract).then_inc(s_lx, 1)
            lo(1)
            for s in range(NS):
                mix(s)
                read(s)
                if s == LAST:
                    merged_lo(3)
                if s + 2 < NS:
                    lo(s + 2)
                late(s)
            dve.wait_ge(s_read_a, ACT_READS[NS - 1])
            dve.tensor_reduce(st_t, st_o, AX_X, ALU.add).then_inc(s_fin_ss, 1)
            dve.wait_ge(s_hx, 3 + KC + 1)
            link(dve.reciprocal(st_r, st_q))
            dve.wait_ge(s_read_v, DVE_READS[NS - 1])
            dve.wait_ge(s_xr, 16)
            for i in range(TT):
                dve.scalar_tensor_tensor(out=OUT[:, i, :], in0=Y[:, i, :], scalar=st_r[:, i:i + 1], in1=XR[:, i, :],
                                         op0=ALU.mult, op1=ALU.add).then_inc(s_fin, 1)

        @block.tensor
        def _(pe):
            def product(s):
                kind, n = SLABS[s][:2]
                pe.wait_ge(s_lo, s + 1)
                if s >= 2:
                    if SLABS[s - 2][0] in BY_ACT:
                        pe.wait_ge(s_read_a, ACT_READS[s - 2])
                    if SLABS[s - 2][0] in BY_DVE:
                        pe.wait_ge(s_read_v, DVE_READS[s - 2])
                ah, al = (bH, bL) if kind == "branch" else (hH, hL)
                wh, wl = WH[:, s % 3], WL[:, s % 2]
                w = width(s)
                for c in range(2):
                    for k in range(KC):
                        if s == 0 and c == 0:
                            pe.wait_ge(s_lx, k + 1)
                        if kind == "branch" and n == 0 and c == 0 and k % 2 == 0:
                            pe.wait_ge(s_blo, 4 * (2 - SLABS[s][4]) + k // 2 + 1)
                        if kind == "out" and n == 0 and c == 0 and k % 2 == 0:
                            pe.wait_ge(s_mlo, k // 2 + 1)
                        if kind in TOKEN_MAJOR:
                            o = bank(s)[:, w * c:w * c + w]
                            pairs = [(a[:, k, P * c:P * c + P], b[:, k, 0:w])
                                     for a, b in ((ah, wl), (al, wh), (ah, wh))]
                        else:
                            o = bank(s)[:, T * c:T * c + T]
                            pairs = [(b[:, k, P * c:P * c + P], a[:, k, :])
                                     for a, b in ((ah, wl), (al, wh), (ah, wh))]
                        for j, (l, r) in enumerate(pairs):
                            mm = pe.matmul(o, l, r, start=(k == 0 and j == 0), stop=(k == KC - 1 and j == 2))
                mm.then_inc(s_prod, 1)

            def hg_scores(u):
                h, i = u // 2, u % 2
                p, hp = h // 2, h % 2
                if i == 0:
                    pe.wait_ge(s_hmul, h + 1)
                if u >= 2:
                    pe.wait_ge(s_hmask, u - 1)
                b0 = 2 + 2 * (u % 2)
                q = QK[p % 2]
                for lv in range(1, 8):
                    b = LEVELS[lv]
                    t = q[:, lv, hp, P * i:P * i + P]
                    up = t.rearrange("p (n w) -> p n w", w=2 * b)[:, :, b:2 * b]
                    pe.matmul(ps[:, b0, 64 * (lv - 1):64 * lv], t, up, start=(lv == 1), stop=(lv == 7))
                mm = pe.matmul(ps[:, b0 + 1, 0:P], ones, HQ[:, h, P * i:P * i + P], start=True, stop=(i == 0))
                if i:
                    mm = pe.matmul(ps[:, b0 + 1, P:2 * P], q[:, 0, hp, 0:P], q[:, 0, hp, P:T], start=False, stop=True)
                mm.then_inc(s_hp, 1)

            def hg_values(u):
                h, i = u // 2, u % 2
                pe.wait_ge(s_hmask, u + 1)
                pe.wait_ge(s_read_v, DVE_READS[WHERE[("hv", h // 2)]])
                if h and i == 0:
                    pe.wait_ge(s_hoc, h)
                o = ps[:, 6, P * i:P * i + P]
                v = HV[:, i, P * h:P * h + P]
                pm = PM[:, u % 2]
                mm = pe.matmul(o, v, pm[:, 0:P], start=True, stop=(i == 0))
                if i:
                    mm = pe.matmul(o, HV[:, 0, P * h:P * h + P], pm[:, P:2 * P], start=False, stop=True)
                mm.then_inc(s_hpv, 1)

            def compress(a):
                pe.wait_ge(s_cw[a], 32)
                pe.wait_ge(s_zero, 2 * a + 2)
                if a:
                    pe.wait_ge(s_ck, 1)
                else:
                    pe.wait_ge(s_hn, HG)
                for k in range(CB):
                    mm = pe.matmul(ps[0:2 * NCMP, 7, 0:P], cpe[:, a, k].rearrange("p g c -> p (g c)"), WC[a][:, k, :],
                                   start=(k == 0), stop=(k == CB - 1))
                mm.then_inc(s_cpe, 1)

            def mix(s):
                if 0 <= s - U0 < NU:
                    hg_scores(s - U0)
                if 0 <= s - U0 - 1 < NU:
                    hg_values(s - U0 - 1)
                for h in range(HG):
                    if s == U0 + 3 + 2 * h:
                        pe.wait_ge(s_hsq, h + 1)
                        if h:
                            pe.wait_ge(s_hrs, h)
                        pe.matmul(ps[:, 7, 0:T], ones, SQ, start=True, stop=True).then_inc(s_hss, 1)
                if s == CK:
                    compress(0)
                if s == CV:
                    pe.wait_ge(s_ck, 1)
                    pe.transpose(ps[:, 6, 0:2 * NCMP], CSB[0:2 * NCMP, 0, :],
                                 ident[0:2 * NCMP, 0:2 * NCMP]).then_inc(s_cpe, 1)
                    compress(1)
                if s == CX:
                    pe.wait_ge(s_cv, 1)
                    pe.wait_ge(s_ckb, 1)
                    for g in range(2):
                        mm = pe.matmul(ps[:, 6, P * g:P * g + P], K[0:2 * NCMP, K_SEL + P * g:K_SEL + P * g + P],
                                       CSB[0:2 * NCMP, 1, :], start=True, stop=True)
                    mm.then_inc(s_cpe, 1)
                if s == SC:
                    pe.wait_ge(s_dup[2], 32)
                    for i in range(TT):
                        for m in range(HEADS // 2):
                            at = 256 * i + 32 * m
                            o = ps[:, 7, at:at + 32].rearrange("p (b c) -> p b c", b=2)[:, :, 0:NCMP]
                            mm = pe.matmul(o, qT[:, m, P * i:P * i + P], CKD[:, m // 2, :, 0:NCMP],
                                           start=(i == 0 and m == 0), stop=(i == TT - 1 and m == HEADS // 2 - 1))
                    mm.then_inc(s_cpe, 1)
                if s == TURN:
                    pe.wait_ge(s_cpc, 1)
                    pe.wait_ge(s_cvd, 1)
                    for g in range(GROUPS):
                        for i in range(TT):
                            mm = pe.transpose(ps[:, 6 + g // 2, 256 * (g % 2) + P * i:256 * (g % 2) + P * i + P],
                                              PC[:, i, 4 * g:4 * g + 4, :].rearrange("p h c -> p (h c)"), ident)
                    mm.then_inc(s_cpe, 1)
                if 0 <= s - H0 < HEADS:
                    at_scores(s - H0)
                if 0 <= s - H0 - 2 < HEADS:
                    at_turn(s - H0 - 2)
                if 0 <= s - H0 - 3 < HEADS:
                    at_values(s - H0 - 3)
                g = s - G0
                if 0 <= g < 4:
                    pe.wait_ge(s_pool, g + 1)
                    pe.wait_ge(s_pw, 64)
                    if g == 0:
                        pe.wait_ge(s_pct, 1)
                    else:
                        pe.wait_ge(s_px, g)
                    for c in range(2):
                        for k in range(2):
                            mm = pe.matmul(ps[:, 7, 256 * c:256 * c + 256], PW[:, g, k, P * c:P * c + P],
                                           BV[:, 2 * g + k, :], start=(k == 0), stop=(k == 1))
                    mm.then_inc(s_pmix, 1)

            def at_scores(h):
                m, hh, g = head(h)
                r = slice(64 * hh, 64 * hh + 64)
                if h == 0:
                    pe.wait_ge(s_dup[0], 32)
                    pe.wait_ge(s_dup[1], 32)
                    pe.wait_ge(s_read_v, DVE_READS[WHERE[("q", 3)]])
                else:
                    pe.wait_ge(s_exp, h)
                for a in range(2):
                    pe.matmul(ps[:, 2, 256 * a:256 * a + 256], qT[r, m, P:T], KD[r, a, g, :],
                              start=(a == 0), stop=False)
                pe.matmul(ps[:, 2, :].rearrange("p (a k) -> p a k", a=2)[:, :, P:T], IB[:],
                          MB[:].rearrange("p (a k) -> p a k", a=1).to_broadcast((P, 2, P)), start=False, stop=True)
                for a in range(2):
                    pe.matmul(ps[:, 3, 128 * a:128 * a + 128], qT[r, m, 0:P], KD[r, a, g, 0:P],
                              start=(a == 0), stop=False)
                pe.matmul(ps[:, 3, 0:256].rearrange("p (a k) -> p a k", a=2), IB[:],
                          MB[:].rearrange("p (a k) -> p a k", a=1).to_broadcast((P, 2, P)),
                          start=False, stop=True).then_inc(s_as, 1)

            def at_turn(h):
                pe.wait_ge(s_scl, h + 1)
                if h:
                    pe.wait_ge(s_apt, h)
                    pe.wait_ge(s_apv2, h)
                pp = PP[:, h % 2]
                o = ps_flat[:, 512 * 4:512 * 4 + 768]
                for a in range(2):
                    pe.transpose(o[:, 384 * a:384 * a + 128], pp[:, 512 + 128 * a:640 + 128 * a], ident)
                    pe.transpose(o[:, 384 * a + 128:384 * a + 256], pp[:, 256 * a:256 * a + 128], ident)
                    mm = pe.transpose(o[:, 384 * a + 256:384 * a + 384], pp[:, 256 * a + 128:256 * a + 256], ident)
                mm.then_inc(s_at, 1)

            def at_values(h):
                m, hh, g = head(h)
                i = h % 4
                pe.wait_ge(s_apt, h + 1)
                pe.wait_ge(s_apv2, h + 1)
                if h == 0:
                    pe.wait_ge(s_pct, 1)
                    pe.wait_ge(s_pct_a, 1)
                if hh == 0 and h:
                    pe.wait_ge(s_aoa, h // 2)
                o = ps[64 * hh:64 * hh + 64, 6, 0:T]
                pe.matmul(o, CVD[:, i, HEAD * g:HEAD * g + HEAD], PCT[:, g, :], start=True, stop=False)
                for a in range(2):
                    pe.matmul(o, VV[:, a, 0, HEAD * g:HEAD * g + HEAD], PTS[:, 384 * a:384 * a + 256],
                              start=False, stop=False)
                    mm = pe.matmul(o[:, P:T], VV[:, a, 1, HEAD * g:HEAD * g + HEAD],
                                   PTS[:, 384 * a + 256:384 * a + 384], start=False, stop=(a == 1))
                mm.then_inc(s_apv, 1)

            pe.wait_ge(s_small, 48)
            for c in range(KC):
                for i in range(TT):
                    pe.wait_ge(s_xn, i + 1)
                    mm = pe.transpose(ps[:, 2 + c // 2, 256 * (c % 2) + P * i:256 * (c % 2) + P * i + P],
                                      xin[:, i, P * c:P * c + P], ident)
                if c % 2:
                    mm.then_inc(s_xt, 1)
            for s in range(NS):
                mix(s)
                product(s)


def tslot(s):
    return s % 2


def constant_table():
    import numpy as np
    k = np.zeros((P, K_ALL + P), np.float32)
    s = np.arange(P)[:, None]
    j = np.arange(64)[None, :]
    for n, b in enumerate(LEVELS[1:]):
        t = (j // b) * 2 * b + b + j % b
        k[:, K_MASK + 64 * n:K_MASK + 64 * n + 64] = (s // (2 * b) == t // (2 * b)) & (s % (2 * b) < b)
    k[:, K_ID:K_ID + P] = np.eye(P)
    k[:, K_ONE:K_ONE + P] = 1.0
    k[:, K_CAUSAL:K_CAUSAL + P] = np.where(np.arange(P)[None, :] <= s, 0.0, -1e30)
    for i in range(TT):
        t = i * P + s
        end = np.arange(NCMP)[None, :] * CS + CB - 1
        k[:, K_CMASK + 15 * i:K_CMASK + 15 * i + 15] = np.where(end <= t, 0.0, -1e30)
        k[:, K_VALID + i] = (t[:, 0] >= CB - 1)
    for g, w in enumerate(WINDOWS):
        k[:, K_COUNT + 16 * g:K_COUNT + 16 * g + 16] = 1.0 / np.minimum(np.arange(16) + 1, w)
    for i in range(4):
        k[32 * i:32 * i + 32, K_ROWS + i] = 1.0
        for g in range(2):
            for c in range(NCMP):
                k[NCMP * g + c, K_SEL + P * g + 32 * i + c] = 1.0
    return k


def kernel(x, pre_norm, w_in, cmp_pe_k, cmp_pe_v, cmp_w_k, cmp_w_v, pool_w, pool_scale,
           hgrn_lb_logits, hgrn_norm, w_branch, w_out, post_norm):
    import numpy as np
    import concourse.bacc as bacc
    from concourse.bass_utils import run_bass_kernel_spmd

    def by_partition(v):
        return np.asarray(v).reshape(KC, P).T

    def twice(pe):
        t = np.asarray(pe)[0].T
        return np.concatenate([t, t], axis=0)

    small = np.ascontiguousarray(np.concatenate(
        [by_partition(pre_norm), by_partition(hgrn_lb_logits), by_partition(hgrn_norm), by_partition(pool_scale),
         twice(cmp_pe_k), twice(cmp_pe_v)], axis=1))
    arrays = {
        "x": np.ascontiguousarray(x), "small": small, "consts": constant_table(),
        "w_in": np.ascontiguousarray(w_in),
        "cmp_w": np.ascontiguousarray(np.concatenate([np.asarray(cmp_w_k), np.asarray(cmp_w_v)], axis=0)),
        "pool_w": np.ascontiguousarray(pool_w), "w_branch": np.ascontiguousarray(w_branch),
        "w_out": np.ascontiguousarray(w_out), "post_norm": np.ascontiguousarray(post_norm),
    }
    nc = bacc.Bacc("TRN2", target_bir_lowering=False, num_devices=1)
    args = [nc.dram_tensor(n, a.shape, mybir.dt.from_np(a.dtype), kind="ExternalInput").ap()
            for n, a in arrays.items()]
    out = nc.dram_tensor("out", (1, T, D), F32, kind="ExternalOutput").ap()
    trunk(nc, *args, out)
    r = run_bass_kernel_spmd(nc, [arrays], core_ids=[0])
    return r.results[0]["out"]
```

```python
from contextlib import ExitStack

import concourse.bass as bass
from concourse import mybir

F32 = mybir.dt.float32
F32R = mybir.dt.float32r
BF16 = mybir.dt.bfloat16
ALU = mybir.AluOpType
ACT = mybir.ActivationFunctionType
AX_X = mybir.AxisListType.X

P = 128
D = 1024
T = 256
KC = D // P
TT = T // P
SLAB = 256
HEADS, HEAD, GROUPS = 16, 64, 4
HPG = HEADS // GROUPS
CB, CS = 32, 16
NCMP = (T - CB) // CS + 1
SCALE = HEAD ** -0.5
HG = 8
EPS = 1e-6
WINDOWS = (2, 4, 8, 16)
LEVELS = (128, 64, 32, 16, 8, 4, 2, 1)

C_Q, C_KC, C_VC, C_KS, C_VS, C_KW, C_VW = 0, 1024, 1280, 1536, 1792, 2048, 2304
C_GATE, C_ASILU, C_BV, C_BSILU = 2560, 2608, 3632, 4656
C_HQ, C_HF, C_HI, C_CSILU, C_MERGE = 5680, 6704, 7728, 8752, 9776
GATES = 3 * HEADS

K_MASK, K_ID, K_ONE = 0, 448, 576
K_CMASK, K_VALID, K_COUNT = 704, 734, 736
K_ROWS, K_ALL = 800, 804
K_CAUSAL = K_ALL
K_SEL = K_CAUSAL + P
K_COLS = K_SEL + GROUPS * P
V_PRE, V_LB, V_HN, V_PS, V_PEK, V_PEV = 0, 8, 16, 24, 32, 64
V_ALL = 96


def plan_slabs():
    out = [("f", n, "in", C_HF + n * SLAB) for n in range(4)]
    for n in range(4):
        out += [("hq", n, "in", C_HQ + n * SLAB), ("hv", n, "in", C_HI + n * SLAB)]
    out += [("kc", 0, "in", C_KC), ("vc", 0, "in", C_VC), ("vs", 0, "in", C_VS), ("vw", 0, "in", C_VW),
            ("gate", 0, "in", C_GATE), ("q", 2, "in", C_Q + 2 * SLAB)]
    out += [("bv", n, "in", C_BV + n * SLAB) for n in range(4)]
    out += [("q", n, "in", C_Q + n * SLAB) for n in (0, 1, 3)]
    out += [("ks", 0, "in", C_KS), ("kw", 0, "in", C_KW)]
    for b, silu in ((2, C_CSILU), (1, C_BSILU), (0, C_ASILU)):
        out += [("silu", n, "in", silu + n * SLAB, b) for n in range(4)]
        for n in range(4):
            out += [("merge", n, "in", C_MERGE + b * D + n * SLAB, b), ("branch", n, b, n * SLAB, b)]
    out += [("out", n, "out", n * SLAB) for n in range(4)]
    return out


SLABS = plan_slabs()
NS = len(SLABS)
LAST = NS - 5
WHERE = {(s[0], s[1]) + tuple(s[4:]): i for i, s in enumerate(SLABS)}
TOKEN_MAJOR = ("hv", "vs", "vw", "out")
BY_ACT = ("f", "gate", "bv", "q", "ks", "kw", "silu", "merge", "out")
BY_DVE = ("hq", "hv", "kc", "vc", "ks", "kw", "vs", "vw", "q", "silu", "branch", "out")
ACT_READS = [sum(x[0] in BY_ACT for x in SLABS[:i + 1]) for i in range(NS)]
DVE_READS = [sum(x[0] in BY_DVE for x in SLABS[:i + 1]) for i in range(NS)]

U0 = 9
CK, CV, CX, SC, TURN = 27, 28, 29, 30, 32
H0 = 30
G0 = 33
NU = HG * TT


def trunk(nc, x, small, consts, w_in, cmp_w, pool_w, w_branch, w_out, post_norm, out):
    ctx = ExitStack()
    with ctx:
        def sb(name, shape, dt=F32):
            return ctx.enter_context(nc.sbuf_tensor(name, shape, dt))

        def sem(name):
            return ctx.enter_context(nc.semaphore(name))

        ps = ctx.enter_context(nc.psum_tensor("ps", [P, 8, 512], F32))
        ps_flat = ps[:].rearrange("p a b -> p (a b)")

        W = sb("W", [P, 3, KC, SLAB])
        WH = sb("WH", [P, 3, KC, SLAB], F32R)
        WL = sb("WL", [P, 2, KC, SLAB], F32R)
        hH = sb("hH", [P, KC, T], F32R)
        hL = sb("hL", [P, KC, T], F32R)
        bH = sb("bH", [P, KC, T], F32R)
        bL = sb("bL", [P, KC, T], F32R)
        with nc.sbuf_tensor("QS1", [P, 8, T], F32R) as QS1, nc.sbuf_tensor("skip", [P, 4, 2048], F32), \
                nc.sbuf_tensor("QS0", [P, 8, T], F32R) as QS0, nc.sbuf_tensor("KS", [P, 2, GROUPS, 2, T], F32R) as KS:
            pass
        R = sb("R", [P, 8, 2048])
        OC = sb("OC", [P, HG, T])
        PM = sb("PM", [P, 2, 640])
        CP = sb("CP", [P, 2048])
        BR = sb("BR", [P, 2, 512])
        VV = sb("VV", [P, 2, TT, SLAB])
        CVD = sb("CVD", [P, 4, GROUPS * HEAD])
        CKS = sb("CKS", [P, 2, GROUPS, 16], F32R)
        TG = sb("TG", [P, 2, 512])
        K = sb("K", [P, K_ALL])
        V = sb("V", [P, V_ALL])
        IB = sb("IB", [P, P], BF16)
        MB = sb("MB", [P, P], BF16)
        GL = sb("GL", [P, T])
        GT = sb("GT", [P, TT, GATES])
        st = sb("st", [P, 176])

        HK = R[:, 0, :].rearrange("p (h t) -> p h t", h=HG)
        HA = R[:, 1, :].rearrange("p (h t) -> p h t", h=HG)
        HQ = R[:, 2, :].rearrange("p (h t) -> p h t", h=HG)
        HV = R[:, 3, :].rearrange("p (i n) -> p i n", i=TT)
        QK = [R[:, 4 + 2 * b:6 + 2 * b, :].rearrange("p a (l h t) -> p (a l) h t", h=2, t=T) for b in range(2)]
        xin = R[:, 4, :].rearrange("p (i n) -> p i n", i=TT)
        sq = R[:, 5, :].rearrange("p (i n) -> p i n", i=TT)
        causal = R[:, 6, 0:P]
        QS = [QS0, QS1]
        BV = HA
        PP = R[:, 2, 0:1536].rearrange("p (a n) -> p a n", a=2)
        M = R[:, 3, :].rearrange("p (c t) -> p c t", c=KC)
        WC = R[:, 4, :].rearrange("p (a j e) -> p a j e", a=2, e=HEAD)
        SEL = R[:, 3, 0:GROUPS * P]
        OA = R[:, 4, :].rearrange("p (c t) -> p c t", c=KC)
        PW = OC[:].rearrange("p h t -> p (h t)").rearrange("p (g k n) -> p g k n", g=4, k=2)
        MX = BV
        WA = R[:, 3, 1024:1536].rearrange("p (c t) -> p c t", c=2)
        WB = R[:, 3, 1536:2048].rearrange("p (c t) -> p c t", c=2)
        XR = R[:, 0, :].rearrange("p (i n) -> p i n", i=TT)
        POST = R[:, 1, 0:D]
        Y = R[:, 4, :].rearrange("p (i n) -> p i n", i=TT)
        OUT = R[:, 6, :].rearrange("p (i n) -> p i n", i=TT)
        SQ = TG[:, 0, 0:T]
        LR = TG[:, 0, T:2 * T]
        RS = TG[:, 1, 0:T]
        PTS = PM[:].rearrange("p a b -> p (a b)")[:, 0:768]
        U = PM[:].rearrange("p a b -> p (a b)")[:, 768:1280]
        cpe = CP[:, 0:1920].rearrange("p (v j g c) -> p v j g c", v=2, g=GROUPS, c=NCMP)
        CSB = R[0:GROUPS * NCMP, 2, 1536:1536 + HEAD]
        SM = CP[:, 1024:1504].rearrange("p (i h c) -> p i h c", i=TT, h=HEADS)
        PC = CP[:, 0:1024].rearrange("p (i h c) -> p i h c", i=TT, h=HEADS)
        PCT = CP[:, 1024:2048].rearrange("p (g t) -> p g t", g=GROUPS)
        ident = K[:, K_ID:K_ID + P]
        ones = K[:, K_ONE:K_ONE + P]
        st_x, st_r = st[:, 0:2], st[:, 2:4]
        st_lb = st[:, 8:48].rearrange("p (a h) -> p a h", a=5)
        st_hn, st_ps = st[:, 48:56], st[:, 56:64]
        st_eps = st[:, 64:65]
        st_nb = st[:, 66:74].rearrange("p (a n) -> p a n", a=2)
        st_sum = st[:, 74:82].rearrange("p (a n) -> p a n", a=2)
        st_w = st[:, 82:90].rearrange("p (a n) -> p a n", a=2)
        st_mx, st_cs = st[:, 90:122], st[:, 122:154]
        st_o = st[:, 154:162].rearrange("p (i n) -> p i n", i=TT)
        st_t, st_q = st[:, 162:164], st[:, 164:166]
        st_t4 = st[:, 166:170]

        s_small, s_x, s_xr, s_post = sem("small_in"), sem("x_in"), sem("xr_in"), sem("post_in")
        s_land = [sem(f"slab_in{i}") for i in range(3)]
        s_cw, s_sel = sem("cmp_w_in"), sem("spread_in")
        s_pw, s_out = sem("pool_w_in"), sem("out_done")
        s_xt, s_prod = sem("x_turned"), sem("slab_product")
        s_hp, s_hpv, s_hss = sem("hg_scores"), sem("hg_values"), sem("hg_squares")
        s_cpe = sem("cmp_pe")
        s_as, s_at, s_apv = sem("at_scores"), sem("at_turned"), sem("at_values")
        s_pmix = sem("pool_mixed")
        s_hi, s_read_a, s_bhi = sem("w_hi"), sem("act_read"), sem("branch_hi")
        s_hx, s_ac = sem("x_hi"), sem("act_chain")
        s_ln, s_hexp, s_hsq, s_hrs = sem("hg_ln"), sem("hg_exp"), sem("hg_sq"), sem("hg_rstd")
        s_cexp, s_exp, s_apt, s_aoa = sem("cmp_exp"), sem("at_exp"), sem("at_pt_act"), sem("at_out")
        s_pct_a, s_gt = sem("pct_act"), sem("gates_turned")
        s_mhi, s_mfin = sem("merged_hi"), sem("merged_done")
        s_lo, s_read_v, s_blo, s_mlo = sem("w_lo"), sem("dve_read"), sem("branch_lo"), sem("merged_lo")
        s_dc, s_init, s_lx, s_xn = sem("dve_chain"), sem("dve_init"), sem("x_lo"), sem("x_normed")
        s_fk, s_scan, s_hmul, s_hmask = sem("f_done"), sem("hg_scan"), sem("hg_mul"), sem("hg_masked")
        s_hoc, s_hn = sem("hg_out"), sem("hg_normed")
        s_ckh, s_ck, s_cv, s_csm, s_cpc, s_pct = sem("ck_hi"), sem("ck_lo"), sem("cv_out"), sem("cmp_sm"), sem("cmp_probs"), sem("pct_dve")
        s_cvd, s_nb, s_aw, s_apv2 = sem("cvd_out"), sem("at_max"), sem("at_weight"), sem("at_pt_dve")
        s_br = sem("branch_out")
        s_px, s_gg = sem("pool_out"), sem("gates_done")
        s_fin, s_lbd, s_fin_ss = sem("final"), sem("lb_ready"), sem("out_squares")
        s_sub, s_scl, s_pool, s_madd = sem("hg_sub"), sem("at_scaled"), sem("pool_in"), sem("merged_add")
        s_pc = sem("pool_chain")

        def slab_source(s):
            kind, n, w, col = SLABS[s][:4]
            src = {"in": w_in[0], "out": w_out[0]}.get(w)
            if src is None:
                src = w_branch[0, w]
            width = GATES if kind == "gate" else SLAB
            return src[:, col:col + width].rearrange("(k p) n -> p k n", p=P), width

        def width(s):
            return GATES if SLABS[s][0] == "gate" else SLAB

        def bank(s):
            return ps[:, s % 2, :]

        def head(h):
            return h // 2, h % 2, h // HPG

        def queries(h, i):
            return QS[h // 8][:, h % 8, P * i:P * i + P]

        ck_out = ps[0:64, 7, 0:GROUPS * NCMP].rearrange("p (g c) -> p g c", g=GROUPS)

        def query_halves(s):
            n = SLABS[s][1]
            q = QS[n // 2][:].rearrange("p (m e) t -> p m e t", e=2)[:, 2 * (n % 2):2 * (n % 2) + 2]
            b = bank(s).rearrange("p (m t) -> p m t", m=2)
            return [(b[64 * e:64 * e + 64], q[64 * e:64 * e + 64, :, e], q[64 - 64 * e:128 - 64 * e, :, e])
                    for e in range(2)]

        def key_halves(s, part):
            a = 0 if SLABS[s][0] == "ks" else 1
            k = KS[:, part, :, a].rearrange("p (m e) t -> p m e t", e=2)
            b = bank(s).rearrange("p (m t) -> p m t", m=2)
            return [(b[64 * e:64 * e + 64], k[64 * e:64 * e + 64, :, e], k[64 - 64 * e:128 - 64 * e, :, e])
                    for e in range(2)]

        block = ctx.enter_context(nc.Block())

        @block.sync
        def _(sp):
            def load_slab(s):
                if s >= 3:
                    sp.wait_ge(s_lo, s - 2)
                src, n = slab_source(s)
                sp.dma_start(W[:, s % 3, :, 0:n], src).then_inc(s_land[s % 3], 16)

            sp.dma_start(xin, x[0].rearrange("(i p) n -> p i n", p=P)).then_inc(s_x, 16)
            sp.dma_start(V[:], small).then_inc(s_small, 16)
            sp.dma_start(K[:], consts[:, 0:K_ALL]).then_inc(s_small, 16)
            sp.dma_start(causal, consts[:, K_CAUSAL:K_CAUSAL + P]).then_inc(s_small, 16)
            for s in range(3):
                load_slab(s)
            for s in range(NS):
                if s + 3 < NS:
                    load_slab(s + 3)
                if s == U0 + 11 + 3:
                    sp.wait_ge(s_hp, 12)
                    for a in range(2):
                        sp.dma_start(WC[:, a], cmp_w[a].rearrange("(j k) d e -> (k d) j e", k=2)).then_inc(s_cw, 16)
                if s == U0 + NU + 2:
                    sp.wait_ge(s_hpv, NU)
                    sp.dma_start(SEL[0:GROUPS * NCMP, :],
                                 consts[0:GROUPS * NCMP, K_SEL:K_SEL + GROUPS * P]).then_inc(s_sel, 16)
                if s == G0 - 2:
                    sp.wait_ge(s_br, 4)
                    for g in range(4):
                        sp.dma_start(PW[:, g], pool_w[0, g].rearrange("(k p) n -> p k n", p=P)).then_inc(s_pw, 16)
                if s == NS - 8:
                    sp.wait_ge(s_as, HEADS)
                    sp.wait_ge(s_br, 8)
                    sp.dma_start(XR, x[0].rearrange("(i p) n -> p i n", p=P)).then_inc(s_xr, 16)
                    sp.dma_start(POST, post_norm.to_broadcast((P, D))).then_inc(s_post, 16)
            for i in range(TT):
                sp.wait_ge(s_fin, i + 1)
                sp.dma_start(out[0, i * P:(i + 1) * P, :], OUT[:, i, :]).then_inc(s_out, 16)
            sp.wait_ge(s_out, 16 * TT)

        @block.gpsimd
        def _(pool):
            chain = [0]

            def link(ins):
                chain[0] += 1
                ins.then_inc(s_pc, 1)
                pool.wait_ge(s_pc, chain[0])

            for p in range(4):
                pool.wait_ge(s_scan, p + 1)
                if p >= 2:
                    pool.wait_ge(s_hp, 4 * (p - 1))
                else:
                    pool.wait_ge(s_xn, 2)
                    pool.wait_ge(s_xt, 4)
                a2 = HA[:, 2 * p:2 * p + 2, :].rearrange("p h t -> p (h t)")
                for i, b in enumerate(LEVELS):
                    n = 2 * T // (2 * b)
                    av = a2.rearrange("p (n w) -> p n w", w=2 * b)
                    dv = QK[p % 2][:, i].rearrange("p h t -> p (h t)").rearrange("p (n w) -> p n w", w=2 * b)
                    edge = av[:, :, b - 1:b].to_broadcast((P, n, b))
                    last = pool.tensor_tensor(dv[:, :, 0:b], edge, av[:, :, 0:b], ALU.subtract)
                    if i:
                        last = pool.tensor_tensor(dv[:, :, b:2 * b], av[:, :, b:2 * b], edge, ALU.subtract)
                last.then_inc(s_sub, 1)
            pool.wait_ge(s_hpv, NU)

            def pool_group(g):
                w = WINDOWS[g]
                src = BV[:, 2 * g:2 * g + 2, :]
                if g == 0:
                    pool.wait_ge(s_read_a, ACT_READS[WHERE[("bv", 3)]])
                else:
                    pool.wait_ge(s_pool, g)
                cur, sh, flip = src, 1, 0
                while sh < w:
                    dst = (WA, WB)[flip]
                    link(pool.tensor_tensor(dst[:, :, sh:T], cur[:, :, sh:T], cur[:, :, 0:T - sh], ALU.add))
                    link(pool.tensor_copy(dst[:, :, 0:sh], cur[:, :, 0:sh]))
                    cur, sh, flip = dst, sh * 2, 1 - flip
                dst = (WA, WB)[flip]
                link(pool.tensor_scalar(dst, cur, 1.0 / w, None, ALU.mult))
                cnt = K[:, K_COUNT + 16 * g:K_COUNT + 16 * g + w].rearrange("p (a n) -> p a n", a=1)
                link(pool.tensor_tensor(dst[:, :, 0:w], cur[:, :, 0:w], cnt.to_broadcast((P, 2, w)), ALU.mult))
                pool.tensor_tensor(src, dst, src, ALU.subtract).then_inc(s_pool, 1)

            def scale_head(h):
                pool.wait_ge(s_aw, h + 1)
                w = st_w[:, h % 2]
                pp = PP[:, h % 2]
                for j in range(2):
                    pool.tensor_scalar(pp[:, 256 * j:256 * j + 256], pp[:, 256 * j:256 * j + 256],
                                       w[:, j:j + 1], None, ALU.mult)
                for j in range(2):
                    last = pool.tensor_scalar(pp[:, 512 + 128 * j:640 + 128 * j], pp[:, 512 + 128 * j:640 + 128 * j],
                                              w[:, 2 + j:3 + j], None, ALU.mult)
                last.then_inc(s_scl, 1)

            def add_merged(b, n):
                k = 4 * (2 - b) + n
                pool.wait_ge(s_read_v, DVE_READS[WHERE[("branch", n, b)]])
                m = M[:, 2 * n:2 * n + 2, :].rearrange("p c t -> p (c t)")
                if b < 2:
                    pool.wait_ge(s_madd, k - 3)
                    pool.tensor_tensor(m, m, U, ALU.add).then_inc(s_madd, 1)
                else:
                    pool.tensor_copy(m, U).then_inc(s_madd, 1)

            for g in range(4):
                pool_group(g)
            for s in range(H0, NS):
                if H0 <= s < H0 + HEADS:
                    scale_head(s - H0)
                if SLABS[s][0] == "branch" and SLABS[s][4]:
                    add_merged(SLABS[s][4], SLABS[s][1])

        @block.scalar
        def _(act):
            chain = [0]

            def link(ins):
                chain[0] += 1
                ins.then_inc(s_ac, 1)
                act.wait_ge(s_ac, chain[0])

            def hi(s):
                act.wait_ge(s_land[s % 3], 16 * (s // 3 + 1))
                if s >= 3:
                    act.wait_ge(s_prod, s - 2)
                n = width(s)
                act.activation(WH[:, s % 3, :, 0:n], W[:, s % 3, :, 0:n], ACT.Copy).then_inc(s_hi, 1)

            def mix(s):
                if s == U0 - 5:
                    for p in range(4):
                        act.wait_ge(s_fk, p + 1)
                        f = OC[:, 2 * p:2 * p + 2, :]
                        act.activation(f, f, ACT.Ln).then_inc(s_ln, 1)
                for p in range(4):
                    if s == U0 - 3 + 4 * p:
                        act.wait_ge(s_sub, p + 1)
                        act.wait_ge(s_scan, p + 1)
                        q = QK[p % 2]
                        act.activation(q[:, 0, :, P:T], HA[:, 2 * p:2 * p + 2, P:T], ACT.Exp)
                        act.activation(q[:, 0, :, 0:P], q[:, 0, :, 0:P], ACT.Exp)
                        act.activation(q[:, 1:8].rearrange("p l h t -> p (l h t)"),
                                       q[:, 1:8].rearrange("p l h t -> p (l h t)"), ACT.Exp).then_inc(s_hexp, 1)
                for h in range(HG):
                    if s == U0 + 2 + 2 * h:
                        act.wait_ge(s_hoc, h + 1)
                        act.activation(SQ, OC[:, h, :], ACT.Square).then_inc(s_hsq, 1)
                    if s == U0 + 3 + 2 * h:
                        act.wait_ge(s_hss, h + 1)
                        if h:
                            act.wait_ge(s_hn, h)
                        link(act.activation(LR, ps[:, 7, 0:T], ACT.Ln, scale=1.0 / P, bias=st_eps))
                        act.activation(RS, LR, ACT.Exp, scale=-0.5).then_inc(s_hrs, 1)
                if s == CK:
                    act.wait_ge(s_cpe, 1)
                    for half in range(2):
                        last = act.activation(CKS[64 * half:64 * half + 64, 0, :, 0:NCMP], ck_out, ACT.Copy)
                    last.then_inc(s_ckh, 1)
                if s == SC:
                    act.wait_ge(s_csm, 1)
                    sm = SM.rearrange("p i h c -> p (i h c)")
                    act.activation(sm, sm, ACT.Exp).then_inc(s_cexp, 1)
                if s == TURN:
                    act.wait_ge(s_cpe, 5)
                    act.activation(PCT[:, 0:2].rearrange("p g t -> p (g t)"), ps[:, 6, :],
                                   ACT.Copy).then_inc(s_pct_a, 1)
                h = s - H0 - 2
                if 0 <= h < HEADS:
                    act.wait_ge(s_at, h + 1)
                    if h:
                        act.wait_ge(s_apv, h)
                    act.activation(PTS[:, 0:512], ps[:, 4, :], ACT.Copy).then_inc(s_apt, 1)
                h = s - H0
                if 0 <= h < HEADS:
                    act.wait_ge(s_nb, h + 1)
                    if h >= 2:
                        act.wait_ge(s_at, h - 1)
                    pp, nb, sm = PP[:, h % 2], st_nb[:, h % 2], st_sum[:, h % 2]
                    for j in range(2):
                        act.activation(pp[:, 256 * j:256 * j + 256], ps[:, 2, 256 * j:256 * j + 256], ACT.Exp,
                                       bias=nb[:, j:j + 1], scale=SCALE, accum_out=sm[:, j:j + 1])
                    for j in range(2):
                        last = act.activation(pp[:, 512 + 128 * j:640 + 128 * j], ps[:, 3, 128 * j:128 * j + 128],
                                              ACT.Exp, bias=nb[:, 2 + j:3 + j], scale=SCALE,
                                              accum_out=sm[:, 2 + j:3 + j])
                    last.then_inc(s_exp, 1)
                h = s - H0 - 3
                if 0 <= h < HEADS and h % 2:
                    act.wait_ge(s_apv, h + 1)
                    act.activation(OA[:, h // 2, :], ps[:, 6, 0:T], ACT.Copy, scale=0.5).then_inc(s_aoa, 1)
                if s >= 1 and SLABS[s - 1][0] == "silu":
                    n, b = SLABS[s - 1][1], SLABS[s - 1][4]
                    k = 4 * (2 - b) + n
                    act.wait_ge(s_br, k + 1)
                    if b < 2:
                        act.wait_ge(s_prod, WHERE[("branch", 3, b + 1)] + 1)
                    act.activation(bH[:, 2 * n:2 * n + 2, :].rearrange("p c t -> p (c t)"), BR[:, k % 2, :],
                                   ACT.Copy).then_inc(s_bhi, 1)
                if s == LAST:
                    for n in range(3):
                        merged_hi(n)

            def merged_hi(n):
                act.wait_ge(s_mfin, n + 1)
                act.wait_ge(s_prod, WHERE[("merge", 3, 0)] + 1)
                act.activation(hH[:, 2 * n:2 * n + 2, :].rearrange("p c t -> p (c t)"),
                               M[:, 2 * n:2 * n + 2, :].rearrange("p c t -> p (c t)"),
                               ACT.Copy, scale=0.5).then_inc(s_mhi, 1)

            def read(s):
                kind, n = SLABS[s][:2]
                if kind not in BY_ACT:
                    return
                act.wait_ge(s_prod, s + 1)
                if kind == "f":
                    act.activation(OC[:, 2 * n:2 * n + 2, :].rearrange("p c t -> p (c t)"), bank(s),
                                   ACT.Sigmoid).then_inc(s_read_a, 1)
                elif kind == "gate":
                    act.activation(GL[0:GATES, :], bank(s)[0:GATES, 0:T], ACT.Tanh, scale=0.5).then_inc(s_read_a, 1)
                elif kind == "bv":
                    act.wait_ge(s_sub, 4)
                    act.activation(BV[:, 2 * n:2 * n + 2, :].rearrange("p c t -> p (c t)"), bank(s),
                                   ACT.Copy).then_inc(s_read_a, 1)
                elif kind == "q":
                    if n < 2:
                        act.wait_ge(s_hp, 12)
                    else:
                        act.wait_ge(s_hmul, 4 * (n - 1))
                    for src, own, other in query_halves(s):
                        last = act.activation(own, src, ACT.Copy)
                    last.then_inc(s_read_a, 1)
                elif kind in ("ks", "kw"):
                    act.wait_ge(s_hp, NU)
                    for src, own, other in key_halves(s, 0):
                        act.activation(own, src, ACT.Copy)
                        last = act.activation(other, src, ACT.Copy)
                    last.then_inc(s_read_a, 1)
                elif kind in ("silu", "merge"):
                    if s == WHERE[("silu", 0, 2)]:
                        act.wait_ge(s_hn, HG)
                    if s >= WHERE[("silu", 2, 2)]:
                        act.wait_ge(s_read_v, DVE_READS[s - 1] - (0 if SLABS[s - 1][0] == "branch" else 1))
                    act.activation(TG[:, tslot(s), :], bank(s), ACT.Tanh, scale=0.5).then_inc(s_read_a, 1)
                else:
                    if n:
                        act.wait_ge(s_read_a, ACT_READS[s - 1])
                    for i in range(TT):
                        last = act.activation(PP[:, i, 0:256], bank(s)[:, 256 * i:256 * i + 256], ACT.Square,
                                              accum_out=st_o[:, i, n:n + 1])
                    last.then_inc(s_read_a, 1)

            act.wait_ge(s_x, 16)
            act.activation(sq[:, 0, :], xin[:, 0, :], ACT.Square, accum_out=st_x[:, 0:1])
            act.activation(sq[:, 1, :], xin[:, 1, :], ACT.Square, accum_out=st_x[:, 1:2]).then_inc(s_hx, 1)
            act.wait_ge(s_hx, 1)
            act.wait_ge(s_init, 1)
            act.activation(st_t, st_x, ACT.Sqrt, scale=1.0 / D, bias=st_eps).then_inc(s_hx, 1)
            act.wait_ge(s_lbd, 1)
            act.activation(st_lb[:, 1], st_lb[:, 0], ACT.Exp).then_inc(s_hx, 1)
            hi(0)
            for c in range(KC):
                act.wait_ge(s_xt, c // 2 + 1)
                act.activation(hH[:, c, :], ps[:, 2 + c // 2, 256 * (c % 2):256 * (c % 2) + 256], ACT.Copy,
                               scale=V[:, V_PRE + c:V_PRE + c + 1]).then_inc(s_hx, 1)
            for s in range(1, 3):
                hi(s)
            for s in range(NS):
                mix(s)
                read(s)
                if s == LAST:
                    merged_hi(3)
                if s + 3 < NS:
                    hi(s + 3)
            act.wait_ge(s_fin_ss, 1)
            act.activation(st_q, st_t, ACT.Sqrt, scale=1.0 / D, bias=st_eps).then_inc(s_hx, 1)

        @block.vector
        def _(dve):
            chain = [0]

            def link(ins):
                chain[0] += 1
                ins.then_inc(s_dc, 1)
                dve.wait_ge(s_dc, chain[0])

            def lo(s):
                dve.wait_ge(s_hi, s + 1)
                if s >= 2:
                    dve.wait_ge(s_prod, s - 1)
                n = width(s)
                dve.tensor_tensor(WL[:, s % 2, :, 0:n], W[:, s % 3, :, 0:n], WH[:, s % 3, :, 0:n],
                                  ALU.subtract).then_inc(s_lo, 1)

            def forget(p):
                dve.wait_ge(s_read_a, ACT_READS[WHERE[("f", p)]])
                for h in range(2 * p, 2 * p + 2):
                    last = dve.tensor_scalar(OC[:, h, :], OC[:, h, :], st_lb[:, 4, h:h + 1], st_lb[:, 3, h:h + 1],
                                             ALU.mult, ALU.add)
                link(last)
                link(dve.tensor_scalar(HK[:, 2 * p:2 * p + 2, :], OC[:, 2 * p:2 * p + 2, :], -1.0, 1.0,
                                       ALU.mult, ALU.add))
                dve.tensor_scalar(OC[:, 2 * p:2 * p + 2, :], OC[:, 2 * p:2 * p + 2, :], 1e-18, None,
                                  ALU.max).then_inc(s_fk, 1)

            def mix(s):
                if 1 <= s <= 4:
                    forget(s - 1)
                if s in (4, 5, 6, 7):
                    p = s - 4
                    dve.wait_ge(s_ln, p + 1)
                    for h in range(2 * p, 2 * p + 2):
                        for i in range(TT):
                            last = dve.tensor_tensor_scan(HA[:, h, i * P:(i + 1) * P], ones,
                                                          OC[:, h, i * P:(i + 1) * P], 0.0, ALU.mult, ALU.add)
                    last.then_inc(s_scan, 1)
                u = s - U0
                if 0 <= u < NU:
                    dve.wait_ge(s_hp, u + 1)
                    if u >= 2:
                        dve.wait_ge(s_hpv, u - 1)
                    b0 = 2 + 2 * (u % 2)
                    n = P * (1 + u % 2)
                    link(dve.tensor_tensor(PM[:, u % 2, 0:n], ps[:, b0 + 1, 0:n], K[:, K_ID:K_ID + n], ALU.mult))
                    for lv in range(1, 8):
                        b = LEVELS[lv]
                        to = PM[:, u % 2, 0:P].rearrange("p (n w) -> p n w", w=2 * b)[:, :, b:2 * b]
                        c = slice(64 * (lv - 1), 64 * lv)
                        last = dve.copy_predicated(to, K[:, c].bitcast(mybir.dt.uint32).rearrange(
                            "p (n w) -> p n w", w=b), ps[:, b0, c].rearrange("p (n w) -> p n w", w=b))
                        if lv < 7:
                            link(last)
                    last.then_inc(s_hmask, 1)
                for h in range(HG):
                    if s == U0 + 2 + 2 * h:
                        dve.wait_ge(s_hpv, 2 * h + 2)
                        dve.tensor_copy(OC[:, h, :], ps[:, 6, 0:T]).then_inc(s_hoc, 1)
                    if s == U0 + 3 + 2 * h:
                        dve.wait_ge(s_hrs, h + 1)
                        dve.scalar_tensor_tensor(out=OC[:, h, :], in0=OC[:, h, :], scalar=st_hn[:, h:h + 1], in1=RS,
                                                 op0=ALU.mult, op1=ALU.mult).then_inc(s_hn, 1)
                for h in range(HG):
                    if s == U0 - 2 + 2 * h:
                        dve.wait_ge(s_hexp, h // 2 + 1)
                        for i, b in enumerate(LEVELS):
                            ev = QK[h // 2 % 2][:, i, h % 2].rearrange("p (n w) -> p n w", w=2 * b)
                            kv = HK[:, h].rearrange("p (n w) -> p n w", w=2 * b)
                            qv = HQ[:, h].rearrange("p (n w) -> p n w", w=2 * b)
                            dve.tensor_tensor(ev[:, :, 0:b], ev[:, :, 0:b], kv[:, :, 0:b], ALU.mult)
                            last = dve.tensor_tensor(ev[:, :, b:2 * b], ev[:, :, b:2 * b], qv[:, :, b:2 * b], ALU.mult)
                        link(last)
                        dve.tensor_tensor(HQ[:, h], HQ[:, h], HK[:, h], ALU.mult).then_inc(s_hmul, 1)
                if s == CK:
                    dve.wait_ge(s_ckh, 1)
                    for half in range(2):
                        last = dve.tensor_tensor(CKS[64 * half:64 * half + 64, 1, :, 0:NCMP], ck_out,
                                                 CKS[0:64, 0, :, 0:NCMP], ALU.subtract)
                    last.then_inc(s_ck, 1)
                if s == CV:
                    dve.wait_ge(s_cpe, 2)
                    dve.tensor_copy(CSB, ps[0:GROUPS * NCMP, 6, 0:HEAD]).then_inc(s_cv, 1)
                if s == CX:
                    link(dve.memset(PC.rearrange("p i h c -> p (i h c)"), 0.0))
                    dve.wait_ge(s_gt, 1)
                    dve.tensor_scalar(GT[:], ps[:, 4, 0:TT * GATES].rearrange("p (i n) -> p i n", i=TT), 1.0, 0.5,
                                      ALU.add, ALU.mult).then_inc(s_gg, 1)
                    dve.wait_ge(s_cpe, 3)
                    for i in range(4):
                        last = dve.tensor_scalar(CVD[:, i, :], ps[:, 6, 0:256], K[:, K_ROWS + i:K_ROWS + i + 1], None,
                                                 ALU.mult)
                    last.then_inc(s_cvd, 1)
                if s == SC:
                    dve.wait_ge(s_cpe, 4)
                    for i in range(TT):
                        sc = ps[:, 7 - i, :].rearrange("p (h b c) -> p b h c", b=2, c=16)
                        cm = K[:, K_CMASK + 15 * i:K_CMASK + 15 * i + 15].rearrange("p (a c) -> p a c", a=1)
                        last = dve.scalar_tensor_tensor(out=SM[:, i], in0=sc[:, 0, :, 0:NCMP], scalar=SCALE,
                                                        in1=cm.to_broadcast((P, HEADS, NCMP)),
                                                        op0=ALU.mult, op1=ALU.add)
                    link(last)
                    for i in range(TT):
                        sc = ps[:, 7 - i, :].rearrange("p (h b c) -> p b h c", b=2, c=16)
                        last = dve.scalar_tensor_tensor(out=SM[:, i], in0=sc[:, 1, :, 0:NCMP], scalar=SCALE,
                                                        in1=SM[:, i], op0=ALU.mult, op1=ALU.add)
                    link(last)
                    smf = SM.rearrange("p i h c -> p (i h) c")
                    link(dve.tensor_reduce(st_mx, smf, AX_X, ALU.max))
                    mxv = st_mx.rearrange("p (h c) -> p h c", c=1)
                    dve.tensor_tensor(smf, smf, mxv.to_broadcast((P, 32, NCMP)), ALU.subtract).then_inc(s_csm, 1)
                if s == SC + 1:
                    dve.wait_ge(s_cexp, 1)
                    dve.wait_ge(s_gg, 1)
                    smf = SM.rearrange("p i h c -> p (i h) c")
                    link(dve.tensor_reduce(st_cs, smf, AX_X, ALU.add))
                    link(dve.tensor_scalar(st_cs, st_cs, 1e-30, None, ALU.max))
                    link(dve.reciprocal(st_cs, st_cs))
                    for i in range(TT):
                        gv = GT[:, i, :].rearrange("p (h j) -> p h j", j=3)[:, :, 0]
                        last = dve.scalar_tensor_tensor(out=st_mx[:, 16 * i:16 * i + 16],
                                                        in0=st_cs[:, 16 * i:16 * i + 16],
                                                        scalar=K[:, K_VALID + i:K_VALID + i + 1], in1=gv,
                                                        op0=ALU.mult, op1=ALU.mult)
                    link(last)
                    mxv = st_mx.rearrange("p (h c) -> p h c", c=1)
                    dve.tensor_tensor(PC.rearrange("p i h c -> p (i h) c")[:, :, 0:NCMP], smf,
                                      mxv.to_broadcast((P, 32, NCMP)), ALU.mult).then_inc(s_cpc, 1)
                if s == TURN:
                    dve.wait_ge(s_cpe, 5)
                    dve.tensor_copy(PCT[:, 2:4].rearrange("p g t -> p (g t)"), ps[:, 7, :]).then_inc(s_pct, 1)
                h = s - H0 - 2
                if 0 <= h < HEADS:
                    dve.wait_ge(s_at, h + 1)
                    if h:
                        dve.wait_ge(s_apv, h)
                    dve.tensor_copy(PTS[:, 512:768], ps[:, 5, 0:256]).then_inc(s_apv2, 1)
                h = s - H0
                if 0 <= h < HEADS:
                    dve.wait_ge(s_as, h + 1)
                    dve.tensor_reduce(st_t4[:, 0:2], ps[:, 2, :].rearrange("p (a k) -> p a k", a=2), AX_X, ALU.max)
                    link(dve.tensor_reduce(st_t4[:, 2:4], ps[:, 3, 0:256].rearrange("p (a k) -> p a k", a=2),
                                           AX_X, ALU.max))
                    dve.tensor_scalar(st_nb[:, h % 2], st_t4, -SCALE, None, ALU.mult).then_inc(s_nb, 1)
                g = s - G0
                if 0 <= g < 4:
                    dve.wait_ge(s_pmix, g + 1)
                    for c in range(2):
                        last = dve.tensor_scalar(MX[:, 2 * g + c, :], ps[:, 7, 256 * c:256 * c + 256],
                                                 st_ps[:, 2 * g + c:2 * g + c + 1], None, ALU.mult)
                    last.then_inc(s_px, 1)
                if s >= 1 and SLABS[s - 1][0] == "silu":
                    n, b = SLABS[s - 1][1], SLABS[s - 1][4]
                    k = 4 * (2 - b) + n
                    dve.wait_ge(s_bhi, k + 1)
                    dve.tensor_tensor(bL[:, 2 * n:2 * n + 2, :].rearrange("p c t -> p (c t)"), BR[:, k % 2, :],
                                      bH[:, 2 * n:2 * n + 2, :].rearrange("p c t -> p (c t)"),
                                      ALU.subtract).then_inc(s_blo, 1)
                if s == LAST:
                    for n in range(3):
                        merged_lo(n)

            def merged_lo(n):
                dve.wait_ge(s_mhi, n + 1)
                dve.scalar_tensor_tensor(out=hL[:, 2 * n:2 * n + 2, :].rearrange("p c t -> p (c t)"),
                                         in0=M[:, 2 * n:2 * n + 2, :].rearrange("p c t -> p (c t)"), scalar=0.5,
                                         in1=hH[:, 2 * n:2 * n + 2, :].rearrange("p c t -> p (c t)"),
                                         op0=ALU.mult, op1=ALU.subtract).then_inc(s_mlo, 1)

            def late(s):
                h = s - H0
                if 0 <= h < HEADS:
                    dve.wait_ge(s_exp, h + 1)
                    if h >= 2:
                        dve.wait_ge(s_scl, h - 1)
                    w = st_w[:, h % 2]
                    link(dve.tensor_scalar(w, st_sum[:, h % 2], 1e-30, None, ALU.max))
                    link(dve.reciprocal(w, w))
                    dve.tensor_tensor(w[:, 0:2], w[:, 0:2], GT[:, 1, 3 * h + 1:3 * h + 3], ALU.mult)
                    dve.tensor_tensor(w[:, 2:4], w[:, 2:4], GT[:, 0, 3 * h + 1:3 * h + 3], ALU.mult)\
                        .then_inc(s_aw, 1)

            def read(s):
                kind, n = SLABS[s][:2]
                if kind not in BY_DVE:
                    return
                dve.wait_ge(s_prod, s + 1)
                if kind in ("q", "ks", "kw", "silu", "branch", "out"):
                    dve.wait_ge(s_read_a, ACT_READS[s if kind != "branch" else s - 1])
                b = bank(s)
                b2 = b.rearrange("p (c t) -> p c t", c=2)
                if kind == "hq":
                    last = dve.tensor_copy(HQ[:, 2 * n:2 * n + 2, :], b2)
                elif kind == "q":
                    for src, own, other in query_halves(s):
                        last = dve.tensor_tensor(other, src, own, ALU.subtract)
                elif kind == "hv":
                    last = dve.tensor_copy(HV[:, :, SLAB * n:SLAB * n + SLAB], b2)
                elif kind in ("kc", "vc"):
                    v = 0 if kind == "kc" else 1
                    pos = V[:, V_PEK + CB * v:V_PEK + CB * v + CB].rearrange("p (r j k) -> p r k j", r=2, k=2)
                    for r in range(2):
                        win = b2[:, :, CS * r:CS * r + CS * NCMP].rearrange("p q (c j k) -> p k j q c", j=CS // 2, k=2)
                        to = cpe[:, v, 8 * r:8 * r + 8].rearrange("p j (q e) c -> p e j q c", e=2)
                        for e in range(2):
                            h = slice(64 * e, 64 * e + 64)
                            for k in range(2):
                                pv = pos[h, r, k].rearrange("p (j q c) -> p j q c", q=1, c=1)
                                last = dve.tensor_tensor(to[64 * k:64 * k + 64, e], win[h, k],
                                                         pv.to_broadcast((64, CS // 2, 2, NCMP)), ALU.add)
                elif kind in ("ks", "kw"):
                    for (src, own, other), (_, hi_own, _) in zip(key_halves(s, 1), key_halves(s, 0)):
                        dve.tensor_tensor(own, src, hi_own, ALU.subtract)
                        last = dve.tensor_tensor(other, src, hi_own, ALU.subtract)
                elif kind in ("vs", "vw"):
                    last = dve.tensor_copy(VV[:, 0 if kind == "vs" else 1], b2)
                elif kind == "silu":
                    br = SLABS[s][4]
                    k = 4 * (2 - br) + n
                    if br < 2 and n == 0:
                        dve.wait_ge(s_madd, 4 * (2 - br))
                    dve.scalar_tensor_tensor(out=U, in0=TG[:, tslot(s), :], scalar=1.0, in1=b, op0=ALU.add,
                                             op1=ALU.mult).then_inc(s_read_v, 1)
                    dve.wait_ge(s_read_v, DVE_READS[s])
                    src = (OA, MX, OC)[br][:, 2 * n:2 * n + 2, :].rearrange("p c t -> p (c t)")
                    if br == 0:
                        dve.wait_ge(s_aoa, HG)
                    if br == 1:
                        dve.wait_ge(s_px, 4)
                    if k >= 2:
                        dve.wait_ge(s_bhi, k - 1)
                    dve.tensor_tensor(BR[:, k % 2, :], src, U, ALU.mult).then_inc(s_br, 1)
                    return
                elif kind == "branch":
                    br = SLABS[s][4]
                    k = 4 * (2 - br) + n
                    if k:
                        dve.wait_ge(s_madd, min(k, 8))
                    if k > 8:
                        dve.wait_ge(s_mfin, k - 8)
                    dve.scalar_tensor_tensor(out=U, in0=TG[:, tslot(s - 1), :], scalar=1.0, in1=b, op0=ALU.add,
                                             op1=ALU.mult).then_inc(s_read_v, 1)
                    if br == 0:
                        dve.wait_ge(s_read_v, DVE_READS[s])
                        m = M[:, 2 * n:2 * n + 2, :].rearrange("p c t -> p (c t)")
                        dve.tensor_tensor(m, m, U, ALU.add).then_inc(s_mfin, 1)
                    return
                elif kind == "out":
                    dve.wait_ge(s_post, 16)
                    pv = POST[:, SLAB * n:SLAB * n + SLAB].rearrange("p (a n) -> p a n", a=1)
                    last = dve.tensor_tensor(Y[:, :, SLAB * n:SLAB * n + SLAB], b2,
                                             pv.to_broadcast((P, TT, SLAB)), ALU.mult)
                last.then_inc(s_read_v, 1)

            dve.memset(st_eps, EPS).then_inc(s_init, 1)
            dve.memset(CKS[:, :, :, NCMP:16].bitcast(F32), 0.0)
            dve.wait_ge(s_small, 48)
            dve.tensor_tensor(st_lb[:, 0], V[:, V_LB:V_LB + 8], V[:, V_LB:V_LB + 8], ALU.subtract).then_inc(s_lbd, 1)
            dve.tensor_copy(IB[:], ident)
            dve.tensor_copy(MB[:], causal)
            dve.tensor_copy(st_hn, V[:, V_HN:V_HN + 8])
            link(dve.tensor_scalar(st_ps, V[:, V_PS:V_PS + 8], 0.5, None, ALU.mult))
            link(dve.tensor_scalar(st_hn, st_hn, 0.5, None, ALU.mult))
            dve.wait_ge(s_hx, 2)
            link(dve.reciprocal(st_r, st_t))
            for i in range(TT):
                dve.tensor_scalar(xin[:, i, :], xin[:, i, :], st_r[:, i:i + 1], None, ALU.mult).then_inc(s_xn, 1)
            dve.wait_ge(s_hx, 3)
            link(dve.reciprocal(st_lb[:, 2], st_lb[:, 1]))
            link(dve.tensor_tensor(st_lb[:, 2], st_lb[:, 2], st_lb[:, 1], ALU.mult))
            link(dve.tensor_tensor(st_lb[:, 3], st_lb[:, 2], st_lb[:, 2], ALU.subtract))
            link(dve.tensor_scalar(st_lb[:, 4], st_lb[:, 3], -1.0, 1.0, ALU.mult, ALU.add))
            lo(0)
            for c in range(KC):
                dve.wait_ge(s_hx, 3 + 2 * (c // 2) + 2)
                dve.scalar_tensor_tensor(out=hL[:, c, :], in0=ps[:, 2 + c // 2, 256 * (c % 2):256 * (c % 2) + 256],
                                         scalar=V[:, V_PRE + c:V_PRE + c + 1], in1=hH[:, c, :],
                                         op0=ALU.mult, op1=ALU.subtract).then_inc(s_lx, 1)
            lo(1)
            for s in range(NS):
                mix(s)
                read(s)
                if s == LAST:
                    merged_lo(3)
                if s + 2 < NS:
                    lo(s + 2)
                late(s)
            dve.wait_ge(s_read_a, ACT_READS[NS - 1])
            dve.tensor_reduce(st_t, st_o, AX_X, ALU.add).then_inc(s_fin_ss, 1)
            dve.wait_ge(s_hx, 3 + KC + 1)
            link(dve.reciprocal(st_r, st_q))
            dve.wait_ge(s_read_v, DVE_READS[NS - 1])
            dve.wait_ge(s_xr, 16)
            for i in range(TT):
                dve.scalar_tensor_tensor(out=OUT[:, i, :], in0=Y[:, i, :], scalar=st_r[:, i:i + 1], in1=XR[:, i, :],
                                         op0=ALU.mult, op1=ALU.add).then_inc(s_fin, 1)

        @block.tensor
        def _(pe):
            def product(s):
                kind, n = SLABS[s][:2]
                pe.wait_ge(s_lo, s + 1)
                if s >= 2:
                    if SLABS[s - 2][0] in BY_ACT:
                        pe.wait_ge(s_read_a, ACT_READS[s - 2])
                    if SLABS[s - 2][0] in BY_DVE:
                        pe.wait_ge(s_read_v, DVE_READS[s - 2])
                ah, al = (bH, bL) if kind == "branch" else (hH, hL)
                wh, wl = WH[:, s % 3], WL[:, s % 2]
                w = width(s)
                for c in range(1 if kind == "gate" else 2):
                    for k in range(KC):
                        if s == 0 and c == 0:
                            pe.wait_ge(s_lx, k + 1)
                        if kind == "branch" and n == 0 and c == 0 and k % 2 == 0:
                            pe.wait_ge(s_blo, 4 * (2 - SLABS[s][4]) + k // 2 + 1)
                        if kind == "out" and n == 0 and c == 0 and k % 2 == 0:
                            pe.wait_ge(s_mlo, k // 2 + 1)
                        if kind in TOKEN_MAJOR:
                            o = bank(s)[:, w * c:w * c + w]
                            pairs = [(a[:, k, P * c:P * c + P], b[:, k, 0:w])
                                     for a, b in ((ah, wl), (al, wh), (ah, wh))]
                        else:
                            o = bank(s)[:, T * c:T * c + T]
                            m = min(w, P)
                            if kind == "gate":
                                o = bank(s)[0:GATES, 0:T]
                            pairs = [(b[:, k, P * c:P * c + m], a[:, k, :])
                                     for a, b in ((ah, wl), (al, wh), (ah, wh))]
                        for j, (l, r) in enumerate(pairs):
                            mm = pe.matmul(o, l, r, start=(k == 0 and j == 0), stop=(k == KC - 1 and j == 2))
                mm.then_inc(s_prod, 1)

            def hg_scores(u):
                h, i = u // 2, u % 2
                p, hp = h // 2, h % 2
                if i == 0:
                    pe.wait_ge(s_hmul, h + 1)
                if u >= 2:
                    pe.wait_ge(s_hmask, u - 1)
                b0 = 2 + 2 * (u % 2)
                q = QK[p % 2]
                for lv in range(1, 8):
                    b = LEVELS[lv]
                    t = q[:, lv, hp, P * i:P * i + P]
                    up = t.rearrange("p (n w) -> p n w", w=2 * b)[:, :, b:2 * b]
                    pe.matmul(ps[:, b0, 64 * (lv - 1):64 * lv], t, up, start=(lv == 1), stop=(lv == 7))
                mm = pe.matmul(ps[:, b0 + 1, 0:P], ones, HQ[:, h, P * i:P * i + P], start=True, stop=(i == 0))
                if i:
                    mm = pe.matmul(ps[:, b0 + 1, P:2 * P], q[:, 0, hp, 0:P], q[:, 0, hp, P:T], start=False, stop=True)
                mm.then_inc(s_hp, 1)

            def hg_values(u):
                h, i = u // 2, u % 2
                pe.wait_ge(s_hmask, u + 1)
                pe.wait_ge(s_read_v, DVE_READS[WHERE[("hv", h // 2)]])
                if h and i == 0:
                    pe.wait_ge(s_hoc, h)
                o = ps[:, 6, P * i:P * i + P]
                v = HV[:, i, P * h:P * h + P]
                pm = PM[:, u % 2]
                mm = pe.matmul(o, v, pm[:, 0:P], start=True, stop=(i == 0))
                if i:
                    mm = pe.matmul(o, HV[:, 0, P * h:P * h + P], pm[:, P:2 * P], start=False, stop=True)
                mm.then_inc(s_hpv, 1)

            def compress(a):
                pe.wait_ge(s_cw, 32)
                pe.wait_ge(s_read_v, DVE_READS[WHERE[("vc", 0)]])
                if a:
                    pe.wait_ge(s_hoc, HG)
                else:
                    pe.wait_ge(s_hrs, HG)
                for j in range(CB // 2):
                    rows = cpe[:, a, j].rearrange("p g c -> p (g c)")
                    if a:
                        mm = pe.matmul(ps[0:GROUPS * NCMP, 6, 0:HEAD], rows, WC[:, a, j, :],
                                       start=(j == 0), stop=(j == CB // 2 - 1))
                    else:
                        mm = pe.matmul(ps[0:HEAD, 7, 0:GROUPS * NCMP], WC[:, a, j, :], rows,
                                       start=(j == 0), stop=(j == CB // 2 - 1))
                mm.then_inc(s_cpe, 1)

            def mix(s):
                if 0 <= s - U0 < NU:
                    hg_scores(s - U0)
                if 0 <= s - U0 - 1 < NU:
                    hg_values(s - U0 - 1)
                for h in range(HG):
                    if s == U0 + 3 + 2 * h:
                        pe.wait_ge(s_hsq, h + 1)
                        if h:
                            pe.wait_ge(s_hrs, h)
                        pe.matmul(ps[:, 7, 0:T], ones, SQ, start=True, stop=True).then_inc(s_hss, 1)
                if s == CK:
                    pe.wait_ge(s_read_a, ACT_READS[WHERE[("gate", 0)]])
                    for i in range(TT):
                        mm = pe.transpose(ps[:, 4, GATES * i:GATES * i + GATES], GL[0:GATES, P * i:P * i + P],
                                          ident[0:GATES, 0:GATES])
                    mm.then_inc(s_gt, 1)
                    compress(0)
                if s == CV:
                    compress(1)
                if s == CX:
                    pe.wait_ge(s_cv, 1)
                    pe.wait_ge(s_sel, 16)
                    for g in range(GROUPS):
                        mm = pe.matmul(ps[:, 6, HEAD * g:HEAD * g + HEAD], SEL[0:GROUPS * NCMP, P * g:P * g + P],
                                       CSB, start=(g == 0), stop=(g == GROUPS - 1))
                    mm.then_inc(s_cpe, 1)
                if s == SC:
                    pe.wait_ge(s_ck, 1)
                    pe.wait_ge(s_cvd, 1)
                    pe.wait_ge(s_read_v, DVE_READS[WHERE[("q", 3)]])
                    for i in range(TT):
                        for h in range(HEADS):
                            mm = pe.matmul(ps[:, 7 - i, 32 * h:32 * h + 32].rearrange("p (b c) -> p b c", b=2),
                                           queries(h, i), CKS[:, :, h // HPG, :], start=(h == 0),
                                           stop=(h == HEADS - 1))
                    mm.then_inc(s_cpe, 1)
                if s == TURN:
                    pe.wait_ge(s_cpc, 1)
                    pe.wait_ge(s_cvd, 1)
                    for g in range(GROUPS):
                        for i in range(TT):
                            mm = pe.transpose(ps[:, 6 + g // 2, 256 * (g % 2) + P * i:256 * (g % 2) + P * i + P],
                                              PC[:, i, 4 * g:4 * g + 4, :].rearrange("p h c -> p (h c)"), ident)
                    mm.then_inc(s_cpe, 1)
                if 0 <= s - H0 - 3 < HEADS:
                    at_values(s - H0 - 3)
                if 0 <= s - H0 - 2 < HEADS:
                    at_turn(s - H0 - 2)
                if 0 <= s - H0 < HEADS:
                    at_scores(s - H0)
                g = s - G0
                if 0 <= g < 4:
                    pe.wait_ge(s_pool, g + 1)
                    pe.wait_ge(s_pw, 64)
                    if g == 0:
                        pe.wait_ge(s_pct, 1)
                    else:
                        pe.wait_ge(s_px, g)
                    for c in range(2):
                        for k in range(2):
                            mm = pe.matmul(ps[:, 7, 256 * c:256 * c + 256], PW[:, g, k, P * c:P * c + P],
                                           BV[:, 2 * g + k, :], start=(k == 0), stop=(k == 1))
                    mm.then_inc(s_pmix, 1)

            def at_scores(h):
                g = h // HPG
                if h == 0:
                    pe.wait_ge(s_read_v, DVE_READS[WHERE[("kw", 0)]])
                else:
                    pe.wait_ge(s_exp, h)
                mask = MB[:].rearrange("p (a k) -> p a k", a=1).to_broadcast((P, 2, P))
                for part in range(2):
                    pe.matmul(ps[:, 2, :], queries(h, 1), KS[:, part, g].rearrange("p a t -> p (a t)"),
                              start=(part == 0), stop=False)
                pe.matmul(ps[:, 2, :].rearrange("p (a k) -> p a k", a=2)[:, :, P:T], IB[:], mask,
                          start=False, stop=True)
                for part in range(2):
                    pe.matmul(ps[:, 3, 0:256].rearrange("p (a k) -> p a k", a=2), queries(h, 0),
                              KS[:, part, g, :, 0:P], start=(part == 0), stop=False)
                pe.matmul(ps[:, 3, 0:256].rearrange("p (a k) -> p a k", a=2), IB[:], mask,
                          start=False, stop=True).then_inc(s_as, 1)

            def at_turn(h):
                pe.wait_ge(s_scl, h + 1)
                if h:
                    pe.wait_ge(s_apt, h)
                    pe.wait_ge(s_apv2, h)
                pp = PP[:, h % 2]
                o = ps_flat[:, 512 * 4:512 * 4 + 768]
                for a in range(2):
                    pe.transpose(o[:, 384 * a:384 * a + 128], pp[:, 512 + 128 * a:640 + 128 * a], ident)
                    pe.transpose(o[:, 384 * a + 128:384 * a + 256], pp[:, 256 * a:256 * a + 128], ident)
                    mm = pe.transpose(o[:, 384 * a + 256:384 * a + 384], pp[:, 256 * a + 128:256 * a + 256], ident)
                mm.then_inc(s_at, 1)

            def at_values(h):
                m, hh, g = head(h)
                i = h % 4
                pe.wait_ge(s_apt, h + 1)
                pe.wait_ge(s_apv2, h + 1)
                if h == 0:
                    pe.wait_ge(s_pct, 1)
                    pe.wait_ge(s_pct_a, 1)
                if hh == 0 and h:
                    pe.wait_ge(s_aoa, h // 2)
                o = ps[64 * hh:64 * hh + 64, 6, 0:T]
                pe.matmul(o, CVD[:, i, HEAD * g:HEAD * g + HEAD], PCT[:, g, :], start=True, stop=False)
                for a in range(2):
                    pe.matmul(o, VV[:, a, 0, HEAD * g:HEAD * g + HEAD], PTS[:, 384 * a:384 * a + 256],
                              start=False, stop=False)
                    mm = pe.matmul(o[:, P:T], VV[:, a, 1, HEAD * g:HEAD * g + HEAD],
                                   PTS[:, 384 * a + 256:384 * a + 384], start=False, stop=(a == 1))
                mm.then_inc(s_apv, 1)

            pe.wait_ge(s_small, 48)
            for c in range(KC):
                for i in range(TT):
                    pe.wait_ge(s_xn, i + 1)
                    mm = pe.transpose(ps[:, 2 + c // 2, 256 * (c % 2) + P * i:256 * (c % 2) + P * i + P],
                                      xin[:, i, P * c:P * c + P], ident)
                if c % 2:
                    mm.then_inc(s_xt, 1)
            for s in range(NS):
                mix(s)
                product(s)


def tslot(s):
    return s % 2


def constant_table():
    import numpy as np
    k = np.zeros((P, K_COLS), np.float32)
    s = np.arange(P)[:, None]
    j = np.arange(64)[None, :]
    for n, b in enumerate(LEVELS[1:]):
        t = (j // b) * 2 * b + b + j % b
        k[:, K_MASK + 64 * n:K_MASK + 64 * n + 64] = (s // (2 * b) == t // (2 * b)) & (s % (2 * b) < b)
    k[:, K_ID:K_ID + P] = np.eye(P)
    k[:, K_ONE:K_ONE + P] = 1.0
    k[:, K_CAUSAL:K_CAUSAL + P] = np.where(np.arange(P)[None, :] <= s, 0.0, -1e30)
    for i in range(TT):
        t = i * P + s
        end = np.arange(NCMP)[None, :] * CS + CB - 1
        k[:, K_CMASK + 15 * i:K_CMASK + 15 * i + 15] = np.where(end <= t, 0.0, -1e30)
        k[:, K_VALID + i] = (t[:, 0] >= CB - 1)
    for g, w in enumerate(WINDOWS):
        k[:, K_COUNT + 16 * g:K_COUNT + 16 * g + 16] = 1.0 / np.minimum(np.arange(16) + 1, w)
    for i in range(4):
        k[32 * i:32 * i + 32, K_ROWS + i] = 1.0
        for g in range(GROUPS):
            for c in range(NCMP):
                k[NCMP * g + c, K_SEL + P * g + 32 * i + c] = 1.0
    return k


def kernel(x, pre_norm, w_in, cmp_pe_k, cmp_pe_v, cmp_w_k, cmp_w_v, pool_w, pool_scale,
           hgrn_lb_logits, hgrn_norm, w_branch, w_out, post_norm):
    import numpy as np
    import concourse.bacc as bacc
    from concourse.bass_utils import run_bass_kernel_spmd

    def by_partition(v):
        return np.asarray(v).reshape(KC, P).T

    def twice(pe):
        t = np.asarray(pe)[0].T
        return np.concatenate([t, t], axis=0)

    small = np.ascontiguousarray(np.concatenate(
        [by_partition(pre_norm), by_partition(hgrn_lb_logits), by_partition(hgrn_norm), by_partition(pool_scale),
         twice(cmp_pe_k), twice(cmp_pe_v)], axis=1))
    arrays = {
        "x": np.ascontiguousarray(x), "small": small, "consts": constant_table(),
        "w_in": np.ascontiguousarray(w_in),
        "cmp_w": np.ascontiguousarray(np.concatenate([np.asarray(cmp_w_k), np.asarray(cmp_w_v)], axis=0)),
        "pool_w": np.ascontiguousarray(pool_w), "w_branch": np.ascontiguousarray(w_branch),
        "w_out": np.ascontiguousarray(w_out), "post_norm": np.ascontiguousarray(post_norm),
    }
    nc = bacc.Bacc("TRN2", target_bir_lowering=False, num_devices=1)
    args = [nc.dram_tensor(n, a.shape, mybir.dt.from_np(a.dtype), kind="ExternalInput").ap()
            for n, a in arrays.items()]
    out = nc.dram_tensor("out", (1, T, D), F32, kind="ExternalOutput").ap()
    trunk(nc, *args, out)
    r = run_bass_kernel_spmd(nc, [arrays], core_ids=[0])
    return r.results[0]["out"]
```

```python
from contextlib import ExitStack

import concourse.bass as bass
from concourse import mybir

F32 = mybir.dt.float32
F32R = mybir.dt.float32r
BF16 = mybir.dt.bfloat16
ALU = mybir.AluOpType
ACT = mybir.ActivationFunctionType
AX_X = mybir.AxisListType.X

P = 128
D = 1024
T = 256
KC = D // P
TT = T // P
SLAB = 256
HEADS, HEAD, GROUPS = 16, 64, 4
HPG = HEADS // GROUPS
CB, CS = 32, 16
NCMP = (T - CB) // CS + 1
SCALE = HEAD ** -0.5
HG = 8
EPS = 1e-6
WINDOWS = (2, 4, 8, 16)
LEVELS = (128, 64, 32, 16, 8, 4, 2, 1)

C_Q, C_KC, C_VC, C_KS, C_VS, C_KW, C_VW = 0, 1024, 1280, 1536, 1792, 2048, 2304
C_GATE, C_ASILU, C_BV, C_BSILU = 2560, 2608, 3632, 4656
C_HQ, C_HF, C_HI, C_CSILU, C_MERGE = 5680, 6704, 7728, 8752, 9776
GATES = 3 * HEADS

K_MASK, K_ID, K_ONE = 0, 448, 576
K_CMASK, K_VALID, K_COUNT = 704, 734, 736
K_ROWS, K_ALL = 800, 804
K_CAUSAL = K_ALL
K_SEL = K_CAUSAL + P
K_COLS = K_SEL + GROUPS * P
V_PRE, V_LB, V_HN, V_PS, V_PEK, V_PEV = 0, 8, 16, 24, 32, 64
V_ALL = 96


def plan_slabs():
    out = [("f", n, "in", C_HF + n * SLAB) for n in range(4)]
    for n in range(4):
        out += [("hq", n, "in", C_HQ + n * SLAB), ("hv", n, "in", C_HI + n * SLAB)]
    out += [("kc", 0, "in", C_KC), ("vc", 0, "in", C_VC), ("vs", 0, "in", C_VS), ("vw", 0, "in", C_VW),
            ("gate", 0, "in", C_GATE), ("q", 2, "in", C_Q + 2 * SLAB)]
    out += [("bv", n, "in", C_BV + n * SLAB) for n in range(4)]
    out += [("q", n, "in", C_Q + n * SLAB) for n in (0, 1, 3)]
    out += [("ks", 0, "in", C_KS), ("kw", 0, "in", C_KW)]
    for b, silu in ((2, C_CSILU), (1, C_BSILU), (0, C_ASILU)):
        out += [("silu", n, "in", silu + n * SLAB, b) for n in range(4)]
        for n in range(4):
            out += [("merge", n, "in", C_MERGE + b * D + n * SLAB, b), ("branch", n, b, n * SLAB, b)]
    out += [("out", n, "out", n * SLAB) for n in range(4)]
    return out


SLABS = plan_slabs()
NS = len(SLABS)
FIRST_A, FIRST_B = 4, 5
LAST = NS - 5
WHERE = {(s[0], s[1]) + tuple(s[4:]): i for i, s in enumerate(SLABS)}
TOKEN_MAJOR = ("hv", "vs", "vw", "out")
BY_ACT = ("f", "gate", "bv", "q", "ks", "kw", "silu", "merge", "out")
BY_DVE = ("hq", "hv", "kc", "vc", "ks", "kw", "vs", "vw", "q", "silu", "branch", "out")
ACT_READS = [sum(x[0] in BY_ACT for x in SLABS[:i + 1]) for i in range(NS)]
DVE_READS = [sum(x[0] in BY_DVE for x in SLABS[:i + 1]) for i in range(NS)]

U0 = 9
CK, CV, CX, SC, TURN = 27, 28, 29, 31, 34
H0 = 32
G0 = 36
NU = HG * TT


def trunk(nc, x, small, consts, w_in, cmp_w, pool_w, w_branch, w_out, post_norm, out):
    ctx = ExitStack()
    with ctx:
        def sb(name, shape, dt=F32):
            return ctx.enter_context(nc.sbuf_tensor(name, shape, dt))

        def sem(name):
            return ctx.enter_context(nc.semaphore(name))

        ps = ctx.enter_context(nc.psum_tensor("ps", [P, 8, 512], F32))
        ps_flat = ps[:].rearrange("p a b -> p (a b)")

        W = sb("W", [P, 3, KC, SLAB])
        WH = sb("WH", [P, 3, KC, SLAB], F32R)
        WL = sb("WL", [P, 2, KC, SLAB], F32R)
        hH = sb("hH", [P, KC, T], F32R)
        hL = sb("hL", [P, KC, T], F32R)
        bH = sb("bH", [P, KC, T], F32R)
        bL = sb("bL", [P, KC, T], F32R)
        with nc.sbuf_tensor("QS1", [P, 8, T], F32R) as QS1, nc.sbuf_tensor("skip", [P, 4, 2048], F32), \
                nc.sbuf_tensor("QS0", [P, 8, T], F32R) as QS0, nc.sbuf_tensor("KS", [P, 2, GROUPS, 2, T], F32R) as KS:
            pass
        R = sb("R", [P, 8, 2048])
        OC = sb("OC", [P, HG, T])
        PM = sb("PM", [P, 2, 640])
        PT1 = sb("PT1", [P, 768])
        CP = sb("CP", [P, 2048])
        BR = sb("BR", [P, 2, 512])
        VV = sb("VV", [P, 2, TT, SLAB])
        CVD = sb("CVD", [P, 4, GROUPS * HEAD])
        CKS = sb("CKS", [P, 2, GROUPS, 16], F32R)
        TG = sb("TG", [P, 2, 512])
        K = sb("K", [P, K_ALL])
        V = sb("V", [P, V_ALL])
        IB = sb("IB", [P, P], BF16)
        MB = sb("MB", [P, P], BF16)
        GL = sb("GL", [P, T])
        GT = sb("GT", [P, TT, GATES])
        st = sb("st", [P, 176])

        HK = R[:, 0, :].rearrange("p (h t) -> p h t", h=HG)
        HA = R[:, 1, :].rearrange("p (h t) -> p h t", h=HG)
        HQ = R[:, 2, :].rearrange("p (h t) -> p h t", h=HG)
        HV = R[:, 3, :].rearrange("p (i n) -> p i n", i=TT)
        QK = [R[:, 4 + 2 * b:6 + 2 * b, :].rearrange("p a (l h t) -> p (a l) h t", h=2, t=T) for b in range(2)]
        xin = R[:, 4, :].rearrange("p (i n) -> p i n", i=TT)
        sq = R[:, 5, :].rearrange("p (i n) -> p i n", i=TT)
        causal = R[:, 6, 0:P]
        QS = [QS0, QS1]
        BV = HA
        PP = R[:, 2, 0:1536].rearrange("p (a n) -> p a n", a=2)
        M = R[:, 3, :].rearrange("p (c t) -> p c t", c=KC)
        WC = R[:, 4, :].rearrange("p (a j e) -> p a j e", a=2, e=HEAD)
        SEL = R[:, 3, 0:GROUPS * P]
        OA = R[:, 4, :].rearrange("p (c t) -> p c t", c=KC)
        PW = OC[:].rearrange("p h t -> p (h t)").rearrange("p (g k n) -> p g k n", g=4, k=2)
        MX = BV
        WA = R[:, 3, 1024:1536].rearrange("p (c t) -> p c t", c=2)
        WB = R[:, 3, 1536:2048].rearrange("p (c t) -> p c t", c=2)
        XR = R[:, 0, :].rearrange("p (i n) -> p i n", i=TT)
        POST = R[:, 1, 0:D]
        Y = R[:, 4, :].rearrange("p (i n) -> p i n", i=TT)
        OUT = R[:, 6, :].rearrange("p (i n) -> p i n", i=TT)
        SQ = TG[:, 0, :].rearrange("p (e t) -> p e t", e=2)
        RS = TG[:, 1, :].rearrange("p (e t) -> p e t", e=2)
        PTS = [PM[:].rearrange("p a b -> p (a b)")[:, 0:768], PT1[:]]
        U = PM[:].rearrange("p a b -> p (a b)")[:, 768:1280]
        cpe = CP[:, 0:1920].rearrange("p (v j g c) -> p v j g c", v=2, g=GROUPS, c=NCMP)
        CSB = R[0:GROUPS * NCMP, 2, 1536:1536 + HEAD]
        SM = CP[:, 1024:1504].rearrange("p (i h c) -> p i h c", i=TT, h=HEADS)
        PC = CP[:, 0:1024].rearrange("p (i h c) -> p i h c", i=TT, h=HEADS)
        PCT = CP[:, 1024:2048].rearrange("p (g t) -> p g t", g=GROUPS)
        ident = K[:, K_ID:K_ID + P]
        ones = K[:, K_ONE:K_ONE + P]
        st_x, st_r = st[:, 0:2], st[:, 2:4]
        st_lb = st[:, 8:48].rearrange("p (a h) -> p a h", a=5)
        st_hn, st_ps = st[:, 48:56], st[:, 56:64]
        st_eps = st[:, 64:65]
        st_nb = st[:, 66:74].rearrange("p (a n) -> p a n", a=2)
        st_sum = st[:, 74:82].rearrange("p (a n) -> p a n", a=2)
        st_w = st[:, 82:90].rearrange("p (a n) -> p a n", a=2)
        st_mx, st_cs = st[:, 90:122], st[:, 122:154]
        st_o = st[:, 154:162].rearrange("p (i n) -> p i n", i=TT)
        st_t, st_q = st[:, 162:164], st[:, 164:166]
        st_t4 = st[:, 166:170]

        s_small, s_consts, s_xr, s_post = sem("small_in"), sem("consts_in"), sem("xr_in"), sem("post_in")
        s_x = [sem(f"x_in{i}") for i in range(TT)]
        s_first, s_hi0a, s_hi0b = sem("first_half_in"), sem("first_hi_act"), sem("first_hi_dve")
        s_lo0, s_lo0p = sem("first_lo"), sem("first_lo_pool")
        s_lbe, s_root, s_last, s_osq = sem("lb_exp"), sem("out_root"), sem("last_product"), sem("last_squares")
        s_land = [sem(f"slab_in{i}") for i in range(3)]
        s_cw, s_sel = sem("cmp_w_in"), sem("spread_in")
        s_pw, s_out = sem("pool_w_in"), sem("out_done")
        s_xt, s_prod = sem("x_turned"), sem("slab_product")
        s_hp, s_hpv, s_hss = sem("hg_scores"), sem("hg_values"), sem("hg_squares")
        s_cpe = sem("cmp_pe")
        s_as, s_at, s_apv = sem("at_scores"), sem("at_turned"), sem("at_values")
        s_pmix = sem("pool_mixed")
        s_hi, s_read_a, s_bhi = sem("w_hi"), sem("act_read"), sem("branch_hi")
        s_hx, s_ac = sem("x_hi"), sem("act_chain")
        s_ln, s_hexp, s_hsq, s_hrs = sem("hg_ln"), sem("hg_exp"), sem("hg_sq"), sem("hg_rstd")
        s_cexp, s_exp, s_apt, s_aoa = sem("cmp_exp"), sem("at_exp"), sem("at_pt_act"), sem("at_out")
        s_pct_a, s_gt = sem("pct_act"), sem("gates_turned")
        s_mhi, s_mfin = sem("merged_hi"), sem("merged_done")
        s_lo, s_read_v, s_blo, s_mlo = sem("w_lo"), sem("dve_read"), sem("branch_lo"), sem("merged_lo")
        s_dc, s_init, s_lx, s_xn = sem("dve_chain"), sem("dve_init"), sem("x_lo"), sem("x_normed")
        s_fk, s_scan, s_hmul, s_hmask = sem("f_done"), sem("hg_scan"), sem("hg_mul"), sem("hg_masked")
        s_hoc, s_hn = sem("hg_out"), sem("hg_normed")
        s_ckh, s_ck, s_cv = sem("ck_hi"), sem("ck_lo"), sem("cv_out")
        s_csm, s_cpc, s_pct = sem("cmp_sm"), sem("cmp_probs"), sem("pct_dve")
        s_cvd, s_nb, s_aw, s_apv2 = sem("cvd_out"), sem("at_max"), sem("at_weight"), sem("at_pt_dve")
        s_br = sem("branch_out")
        s_px, s_gg = sem("pool_out"), sem("gates_done")
        s_fin, s_lbd, s_fin_ss = sem("final"), sem("lb_ready"), sem("out_squares")
        s_sub, s_scl, s_pool, s_madd = sem("hg_sub"), sem("at_scaled"), sem("pool_in"), sem("merged_add")
        s_pc = sem("pool_chain")

        def slab_source(s):
            kind, n, w, col = SLABS[s][:4]
            src = {"in": w_in[0], "out": w_out[0]}.get(w)
            if src is None:
                src = w_branch[0, w]
            width = GATES if kind == "gate" else SLAB
            return src[:, col:col + width].rearrange("(k p) n -> p k n", p=P), width

        def width(s):
            return GATES if SLABS[s][0] == "gate" else SLAB

        def bank(s):
            return ps[:, s % 2, :]

        def head(h):
            return h // 2, h % 2, h // HPG

        def queries(h, i):
            return QS[h // 8][:, h % 8, P * i:P * i + P]

        def last_rows(i):
            return ps[:, (NS - 1) % 2 if i == 0 else 2, 0:SLAB]

        ck_out = ps[0:64, 5, 0:GROUPS * NCMP].rearrange("p (g c) -> p g c", g=GROUPS)

        def query_halves(s):
            n = SLABS[s][1]
            q = QS[n // 2][:].rearrange("p (m e) t -> p m e t", e=2)[:, 2 * (n % 2):2 * (n % 2) + 2]
            b = bank(s).rearrange("p (m t) -> p m t", m=2)
            return [(b[64 * e:64 * e + 64], q[64 * e:64 * e + 64, :, e], q[64 - 64 * e:128 - 64 * e, :, e])
                    for e in range(2)]

        def key_halves(s, part):
            a = 0 if SLABS[s][0] == "ks" else 1
            k = KS[:, part, :, a].rearrange("p (m e) t -> p m e t", e=2)
            b = bank(s).rearrange("p (m t) -> p m t", m=2)
            return [(b[64 * e:64 * e + 64], k[64 * e:64 * e + 64, :, e], k[64 - 64 * e:128 - 64 * e, :, e])
                    for e in range(2)]

        block = ctx.enter_context(nc.Block())

        @block.sync
        def _(sp):
            def load_slab(s):
                if s >= 3:
                    sp.wait_ge(s_lo, s - 2)
                if s == 3:
                    sp.wait_ge(s_lo0p, 1)
                src, n = slab_source(s)
                sp.dma_start(W[:, s % 3, :, 0:n], src).then_inc(s_land[s % 3], 16)

            for i in range(TT):
                sp.dma_start(xin[:, i, :], x[0, P * i:P * i + P, :]).then_inc(s_x[i], 16)
            src = slab_source(0)[0]
            sp.dma_start(W[:, 0, 0:FIRST_A, :], src[:, 0:FIRST_A, :]).then_inc(s_first, 16)
            sp.dma_start(W[:, 0, FIRST_A:KC, :], src[:, FIRST_A:KC, :]).then_inc(s_land[0], 16)
            load_slab(1)
            load_slab(2)
            sp.dma_start(K[:, 0:K_ID], consts[:, 0:K_ID]).then_inc(s_consts, 16)
            sp.dma_start(K[:, K_CMASK:K_ALL], consts[:, K_CMASK:K_ALL]).then_inc(s_consts, 16)
            sp.dma_start(causal, consts[:, K_CAUSAL:K_CAUSAL + P]).then_inc(s_consts, 16)
            for s in range(NS):
                if s + 3 < NS:
                    load_slab(s + 3)
                if s == U0 + 11 + 3:
                    sp.wait_ge(s_hp, 12)
                    for a in range(2):
                        sp.dma_start(WC[:, a], cmp_w[a].rearrange("(j k) d e -> (k d) j e", k=2)).then_inc(s_cw, 16)
                if s == U0 + NU + 2:
                    sp.wait_ge(s_hpv, NU)
                    sp.dma_start(SEL[0:GROUPS * NCMP, :],
                                 consts[0:GROUPS * NCMP, K_SEL:K_SEL + GROUPS * P]).then_inc(s_sel, 16)
                if s == G0 - 2:
                    sp.wait_ge(s_br, 4)
                    for g in range(4):
                        sp.dma_start(PW[:, g], pool_w[0, g].rearrange("(k p) n -> p k n", p=P)).then_inc(s_pw, 16)
                if s == NS - 8:
                    sp.wait_ge(s_as, HEADS)
                    sp.wait_ge(s_br, 8)
                    sp.dma_start(XR, x[0].rearrange("(i p) n -> p i n", p=P)).then_inc(s_xr, 16)
                    sp.dma_start(POST, post_norm.to_broadcast((P, D))).then_inc(s_post, 16)
            for i in range(TT):
                for half in range(2):
                    n = slice(D // 2 * half, D // 2 * half + D // 2)
                    sp.wait_ge(s_fin, 2 * i + half + 1)
                    sp.dma_start(out[0, i * P:(i + 1) * P, n], OUT[:, i, n]).then_inc(s_out, 16)
            sp.wait_ge(s_out, 16 * 2 * TT)

        @block.gpsimd
        def _(pool):
            chain = [0]

            def link(ins):
                chain[0] += 1
                ins.then_inc(s_pc, 1)
                pool.wait_ge(s_pc, chain[0])

            pool.wait_ge(s_hi0b, 1)
            pool.tensor_tensor(WL[:, 0, FIRST_B:KC, :], W[:, 0, FIRST_B:KC, :], WH[:, 0, FIRST_B:KC, :],
                               ALU.subtract).then_inc(s_lo0p, 1)
            for p in range(4):
                pool.wait_ge(s_scan, p + 1)
                if p >= 2:
                    pool.wait_ge(s_hp, 4 * (p - 1))
                else:
                    pool.wait_ge(s_xn, 3)
                    pool.wait_ge(s_xt, 4)
                a2 = HA[:, 2 * p:2 * p + 2, :].rearrange("p h t -> p (h t)")
                for i, b in enumerate(LEVELS):
                    n = 2 * T // (2 * b)
                    av = a2.rearrange("p (n w) -> p n w", w=2 * b)
                    dv = QK[p % 2][:, i].rearrange("p h t -> p (h t)").rearrange("p (n w) -> p n w", w=2 * b)
                    edge = av[:, :, b - 1:b].to_broadcast((P, n, b))
                    last = pool.tensor_tensor(dv[:, :, 0:b], edge, av[:, :, 0:b], ALU.subtract)
                    if i:
                        last = pool.tensor_tensor(dv[:, :, b:2 * b], av[:, :, b:2 * b], edge, ALU.subtract)
                last.then_inc(s_sub, 1)
            pool.wait_ge(s_hpv, NU)

            def pool_group(g):
                w = WINDOWS[g]
                src = BV[:, 2 * g:2 * g + 2, :]
                if g == 0:
                    pool.wait_ge(s_read_a, ACT_READS[WHERE[("bv", 3)]])
                else:
                    pool.wait_ge(s_pool, g)
                cur, sh, flip = src, 1, 0
                while sh < w:
                    dst = (WA, WB)[flip]
                    link(pool.tensor_tensor(dst[:, :, sh:T], cur[:, :, sh:T], cur[:, :, 0:T - sh], ALU.add))
                    link(pool.tensor_copy(dst[:, :, 0:sh], cur[:, :, 0:sh]))
                    cur, sh, flip = dst, sh * 2, 1 - flip
                dst = (WA, WB)[flip]
                link(pool.tensor_scalar(dst, cur, 1.0 / w, None, ALU.mult))
                cnt = K[:, K_COUNT + 16 * g:K_COUNT + 16 * g + w].rearrange("p (a n) -> p a n", a=1)
                link(pool.tensor_tensor(dst[:, :, 0:w], cur[:, :, 0:w], cnt.to_broadcast((P, 2, w)), ALU.mult))
                pool.tensor_tensor(src, dst, src, ALU.subtract).then_inc(s_pool, 1)

            def scale_head(h):
                pool.wait_ge(s_aw, h + 1)
                w = st_w[:, h % 2]
                pp = PP[:, h % 2]
                for j in range(2):
                    pool.tensor_scalar(pp[:, 256 * j:256 * j + 256], pp[:, 256 * j:256 * j + 256],
                                       w[:, j:j + 1], None, ALU.mult)
                for j in range(2):
                    last = pool.tensor_scalar(pp[:, 512 + 128 * j:640 + 128 * j], pp[:, 512 + 128 * j:640 + 128 * j],
                                              w[:, 2 + j:3 + j], None, ALU.mult)
                last.then_inc(s_scl, 1)

            def add_merged(b, n):
                k = 4 * (2 - b) + n
                pool.wait_ge(s_read_v, DVE_READS[WHERE[("branch", n, b)]])
                m = M[:, 2 * n:2 * n + 2, :].rearrange("p c t -> p (c t)")
                if b < 2:
                    pool.wait_ge(s_madd, k - 3)
                    pool.tensor_tensor(m, m, U, ALU.add).then_inc(s_madd, 1)
                else:
                    pool.tensor_copy(m, U).then_inc(s_madd, 1)

            for g in range(4):
                pool_group(g)
            for s in range(H0, NS):
                if H0 <= s < H0 + HEADS:
                    scale_head(s - H0)
                if SLABS[s][0] == "branch" and SLABS[s][4]:
                    add_merged(SLABS[s][4], SLABS[s][1])

        @block.scalar
        def _(act):
            chain = [0]

            def link(ins):
                chain[0] += 1
                ins.then_inc(s_ac, 1)
                act.wait_ge(s_ac, chain[0])

            def hi(s):
                act.wait_ge(s_land[s % 3], 16 * (s // 3 + 1))
                if s >= 3:
                    act.wait_ge(s_prod, s - 2)
                n = width(s)
                act.activation(WH[:, s % 3, :, 0:n], W[:, s % 3, :, 0:n], ACT.Copy).then_inc(s_hi, 1)

            def mix(s):
                if s == U0 - 5:
                    for p in range(4):
                        act.wait_ge(s_fk, p + 1)
                        f = OC[:, 2 * p:2 * p + 2, :]
                        act.activation(f, f, ACT.Ln).then_inc(s_ln, 1)
                for p in range(4):
                    if s == U0 - 3 + 4 * p:
                        act.wait_ge(s_sub, p + 1)
                        act.wait_ge(s_scan, p + 1)
                        q = QK[p % 2]
                        act.activation(q[:, 0, :, P:T], HA[:, 2 * p:2 * p + 2, P:T], ACT.Exp)
                        act.activation(q[:, 0, :, 0:P], q[:, 0, :, 0:P], ACT.Exp)
                        act.activation(q[:, 1:8].rearrange("p l h t -> p (l h t)"),
                                       q[:, 1:8].rearrange("p l h t -> p (l h t)"), ACT.Exp).then_inc(s_hexp, 1)
                for h in range(HG):
                    if s == U0 + 2 + 2 * h:
                        act.wait_ge(s_hoc, h + 1)
                        act.activation(SQ[:, h % 2], OC[:, h, :], ACT.Square).then_inc(s_hsq, 1)
                for p in range(HG // 2):
                    if s == U0 + 5 + 4 * p:
                        act.wait_ge(s_hss, p + 1)
                        if p:
                            act.wait_ge(s_hn, 2 * p)
                        rs = RS.rearrange("p e t -> p (e t)")
                        link(act.activation(rs, ps[:, 7, :], ACT.Ln, scale=1.0 / P, bias=st_eps))
                        act.activation(rs, rs, ACT.Exp, scale=-0.5).then_inc(s_hrs, 1)
                if s == CK:
                    act.wait_ge(s_cpe, 1)
                    for half in range(2):
                        last = act.activation(CKS[64 * half:64 * half + 64, 0, :, 0:NCMP], ck_out, ACT.Copy)
                    last.then_inc(s_ckh, 1)
                if s == TURN:
                    act.wait_ge(s_cpe, 5)
                    act.activation(PCT[:, 0:2].rearrange("p g t -> p (g t)"), ps[:, 6, :],
                                   ACT.Copy).then_inc(s_pct_a, 1)
                h = s - H0 - 2
                if 0 <= h < HEADS:
                    act.wait_ge(s_at, h + 1)
                    if h >= 2:
                        act.wait_ge(s_apv, h // 2)
                    act.activation(PTS[h % 2][:, 0:512], ps[:, 4, :], ACT.Copy).then_inc(s_apt, 1)
                h = s - H0 - 3
                if 0 <= h < HEADS and h % 2:
                    act.wait_ge(s_apv, h // 2 + 1)
                    act.activation(OA[:, h // 2, :], ps[:, 6, 0:T], ACT.Copy, scale=0.5).then_inc(s_aoa, 1)
                h = s - H0
                if 0 <= h < HEADS:
                    act.wait_ge(s_nb, h + 1)
                    if h >= 2:
                        act.wait_ge(s_at, h - 1)
                    pp, nb, sm = PP[:, h % 2], st_nb[:, h % 2], st_sum[:, h % 2]
                    for j in range(2):
                        act.activation(pp[:, 256 * j:256 * j + 256], ps[:, 2, 256 * j:256 * j + 256], ACT.Exp,
                                       bias=nb[:, j:j + 1], scale=SCALE, accum_out=sm[:, j:j + 1])
                    for j in range(2):
                        last = act.activation(pp[:, 512 + 128 * j:640 + 128 * j], ps[:, 3, 128 * j:128 * j + 128],
                                              ACT.Exp, bias=nb[:, 2 + j:3 + j], scale=SCALE,
                                              accum_out=sm[:, 2 + j:3 + j])
                    last.then_inc(s_exp, 1)
                if s == SC + 1:
                    act.wait_ge(s_csm, 1)
                    sm = SM.rearrange("p i h c -> p (i h c)")
                    act.activation(sm, sm, ACT.Exp).then_inc(s_cexp, 1)
                if s >= 1 and SLABS[s - 1][0] == "silu":
                    n, b = SLABS[s - 1][1], SLABS[s - 1][4]
                    k = 4 * (2 - b) + n
                    act.wait_ge(s_br, k + 1)
                    if b < 2:
                        act.wait_ge(s_prod, WHERE[("branch", 3, b + 1)] + 1)
                    act.activation(bH[:, 2 * n:2 * n + 2, :].rearrange("p c t -> p (c t)"), BR[:, k % 2, :],
                                   ACT.Copy).then_inc(s_bhi, 1)
                if s == LAST:
                    for n in range(3):
                        merged_hi(n)

            def merged_hi(n):
                act.wait_ge(s_mfin, n + 1)
                act.wait_ge(s_prod, WHERE[("merge", 3, 0)] + 1)
                act.activation(hH[:, 2 * n:2 * n + 2, :].rearrange("p c t -> p (c t)"),
                               M[:, 2 * n:2 * n + 2, :].rearrange("p c t -> p (c t)"),
                               ACT.Copy, scale=0.5).then_inc(s_mhi, 1)

            def read(s):
                kind, n = SLABS[s][:2]
                if kind not in BY_ACT:
                    return
                act.wait_ge(s_prod, s + 1)
                if kind == "f":
                    act.activation(OC[:, 2 * n:2 * n + 2, :].rearrange("p c t -> p (c t)"), bank(s),
                                   ACT.Sigmoid).then_inc(s_read_a, 1)
                elif kind == "gate":
                    act.activation(GL[0:GATES, :], bank(s)[0:GATES, 0:T], ACT.Tanh, scale=0.5).then_inc(s_read_a, 1)
                elif kind == "bv":
                    act.wait_ge(s_sub, 4)
                    act.activation(BV[:, 2 * n:2 * n + 2, :].rearrange("p c t -> p (c t)"), bank(s),
                                   ACT.Copy).then_inc(s_read_a, 1)
                elif kind == "q":
                    if n < 2:
                        act.wait_ge(s_hp, 12)
                    else:
                        act.wait_ge(s_hmul, 4 * (n - 1))
                    for src, own, other in query_halves(s):
                        last = act.activation(own, src, ACT.Copy)
                    last.then_inc(s_read_a, 1)
                elif kind in ("ks", "kw"):
                    act.wait_ge(s_hp, NU)
                    for src, own, other in key_halves(s, 0):
                        act.activation(own, src, ACT.Copy)
                        last = act.activation(other, src, ACT.Copy)
                    last.then_inc(s_read_a, 1)
                elif kind in ("silu", "merge"):
                    if s == WHERE[("silu", 0, 2)]:
                        act.wait_ge(s_hn, HG)
                    if s >= WHERE[("silu", 2, 2)]:
                        act.wait_ge(s_read_v, DVE_READS[s - 1] - (0 if SLABS[s - 1][0] == "branch" else 1))
                    act.activation(TG[:, tslot(s), :], bank(s), ACT.Tanh, scale=0.5).then_inc(s_read_a, 1)
                else:
                    if n:
                        act.wait_ge(s_read_a, ACT_READS[s - 1])
                    else:
                        act.activation(st_q[:, 0:1], st_eps, ACT.Sqrt)
                    for i in range(TT):
                        last = act.activation(PP[:, i, 0:256], bank(s)[:, 256 * i:256 * i + 256], ACT.Square,
                                              accum_out=st_o[:, i, n:n + 1])
                    last.then_inc(s_read_a, 1)

            act.dma_start(K[:, K_ID:K_CMASK], consts[:, K_ID:K_CMASK]).then_inc(s_small, 16)
            act.dma_start(V[:], small).then_inc(s_small, 16)
            act.wait_ge(s_init, 1)
            act.activation(st_q[:, 0:1], st_eps, ACT.Sqrt)
            for i in range(TT):
                act.wait_ge(s_x[i], 16)
                link(act.activation(sq[:, i, :], xin[:, i, :], ACT.Square, accum_out=st_x[:, i:i + 1]))
                act.activation(st_t[:, i:i + 1], st_x[:, i:i + 1], ACT.Sqrt, scale=1.0 / D,
                               bias=st_eps).then_inc(s_hx, 1)
            act.wait_ge(s_first, 16)
            act.activation(WH[:, 0, 0:FIRST_A, :], W[:, 0, 0:FIRST_A, :], ACT.Copy).then_inc(s_hi0a, 1)
            act.wait_ge(s_small, 32)
            for c in range(KC):
                act.wait_ge(s_xt, c // 2 + 1)
                act.activation(hH[:, c, :], ps[:, 2 + c // 2, 256 * (c % 2):256 * (c % 2) + 256], ACT.Copy,
                               scale=V[:, V_PRE + c:V_PRE + c + 1]).then_inc(s_hx, 1)
            hi(1)
            act.wait_ge(s_lbd, 1)
            act.activation(st_lb[:, 1], st_lb[:, 0], ACT.Exp).then_inc(s_lbe, 1)
            hi(2)
            for s in range(NS - 1):
                mix(s)
                read(s)
                if s == LAST:
                    merged_hi(3)
                if s + 3 < NS:
                    hi(s + 3)
            act.wait_ge(s_read_a, ACT_READS[NS - 2])
            for i in range(TT):
                act.wait_ge(s_last, i + 1)
                act.activation(PP[:, i, 0:256], last_rows(i), ACT.Square, accum_out=st_o[:, i, 3:4]).then_inc(s_osq, 1)
                act.wait_ge(s_fin_ss, i + 1)
                act.activation(st_q[:, i:i + 1], st_t[:, i:i + 1], ACT.Sqrt, scale=1.0 / D,
                               bias=st_eps).then_inc(s_root, 1)

        @block.vector
        def _(dve):
            chain = [0]

            def link(ins):
                chain[0] += 1
                ins.then_inc(s_dc, 1)
                dve.wait_ge(s_dc, chain[0])

            def lo(s):
                dve.wait_ge(s_hi, s)
                if s >= 2:
                    dve.wait_ge(s_prod, s - 1)
                n = width(s)
                dve.tensor_tensor(WL[:, s % 2, :, 0:n], W[:, s % 3, :, 0:n], WH[:, s % 3, :, 0:n],
                                  ALU.subtract).then_inc(s_lo, 1)

            def forget(p):
                dve.wait_ge(s_read_a, ACT_READS[WHERE[("f", p)]])
                for h in range(2 * p, 2 * p + 2):
                    last = dve.tensor_scalar(OC[:, h, :], OC[:, h, :], st_lb[:, 4, h:h + 1], st_lb[:, 3, h:h + 1],
                                             ALU.mult, ALU.add)
                link(last)
                link(dve.tensor_scalar(HK[:, 2 * p:2 * p + 2, :], OC[:, 2 * p:2 * p + 2, :], -1.0, 1.0,
                                       ALU.mult, ALU.add))
                dve.tensor_scalar(OC[:, 2 * p:2 * p + 2, :], OC[:, 2 * p:2 * p + 2, :], 1e-18, None,
                                  ALU.max).then_inc(s_fk, 1)

            def mix(s):
                if 1 <= s <= 4:
                    forget(s - 1)
                if s in (4, 5, 6, 7):
                    p = s - 4
                    dve.wait_ge(s_ln, p + 1)
                    for h in range(2 * p, 2 * p + 2):
                        for i in range(TT):
                            last = dve.tensor_tensor_scan(HA[:, h, i * P:(i + 1) * P], ones,
                                                          OC[:, h, i * P:(i + 1) * P], 0.0, ALU.mult, ALU.add)
                    last.then_inc(s_scan, 1)
                for h in range(HG):
                    if s == U0 + 2 + 2 * h:
                        dve.wait_ge(s_hpv, 2 * h + 2)
                        dve.tensor_copy(OC[:, h, :], ps[:, 6, 0:T]).then_inc(s_hoc, 1)
                    if s == U0 + 5 + 4 * (h // 2):
                        dve.wait_ge(s_hrs, h // 2 + 1)
                        dve.scalar_tensor_tensor(out=OC[:, h, :], in0=OC[:, h, :], scalar=st_hn[:, h:h + 1], in1=RS[:, h % 2],
                                                 op0=ALU.mult, op1=ALU.mult).then_inc(s_hn, 1)
                for h in range(HG):
                    if s == U0 - 2 + 2 * h:
                        dve.wait_ge(s_hexp, h // 2 + 1)
                        for i, b in enumerate(LEVELS):
                            ev = QK[h // 2 % 2][:, i, h % 2].rearrange("p (n w) -> p n w", w=2 * b)
                            kv = HK[:, h].rearrange("p (n w) -> p n w", w=2 * b)
                            qv = HQ[:, h].rearrange("p (n w) -> p n w", w=2 * b)
                            dve.tensor_tensor(ev[:, :, 0:b], ev[:, :, 0:b], kv[:, :, 0:b], ALU.mult)
                            last = dve.tensor_tensor(ev[:, :, b:2 * b], ev[:, :, b:2 * b], qv[:, :, b:2 * b], ALU.mult)
                        link(last)
                        dve.tensor_tensor(HQ[:, h], HQ[:, h], HK[:, h], ALU.mult).then_inc(s_hmul, 1)
                if s == CK:
                    dve.wait_ge(s_ckh, 1)
                    for half in range(2):
                        last = dve.tensor_tensor(CKS[64 * half:64 * half + 64, 1, :, 0:NCMP], ck_out,
                                                 CKS[0:64, 0, :, 0:NCMP], ALU.subtract)
                    last.then_inc(s_ck, 1)
                if s == CV:
                    dve.wait_ge(s_cpe, 2)
                    dve.tensor_copy(CSB, ps[0:GROUPS * NCMP, 6, 0:HEAD]).then_inc(s_cv, 1)
                if s == CX:
                    link(dve.memset(PC.rearrange("p i h c -> p (i h c)"), 0.0))
                    dve.wait_ge(s_gt, 1)
                    dve.tensor_scalar(GT[:], ps[:, 4, 0:TT * GATES].rearrange("p (i n) -> p i n", i=TT), 1.0, 0.5,
                                      ALU.add, ALU.mult).then_inc(s_gg, 1)
                    dve.wait_ge(s_cpe, 3)
                    for i in range(4):
                        last = dve.tensor_scalar(CVD[:, i, :], ps[:, 6, 0:256], K[:, K_ROWS + i:K_ROWS + i + 1], None,
                                                 ALU.mult)
                    last.then_inc(s_cvd, 1)
                if s == TURN:
                    dve.wait_ge(s_cpe, 5)
                    dve.tensor_copy(PCT[:, 2:4].rearrange("p g t -> p (g t)"), ps[:, 7, :]).then_inc(s_pct, 1)
                g = s - G0
                if 0 <= g < 4:
                    dve.wait_ge(s_pmix, g + 1)
                    for c in range(2):
                        last = dve.tensor_scalar(MX[:, 2 * g + c, :], ps[:, 7, 256 * c:256 * c + 256],
                                                 st_ps[:, 2 * g + c:2 * g + c + 1], None, ALU.mult)
                    last.then_inc(s_px, 1)
                if s >= 1 and SLABS[s - 1][0] == "silu":
                    n, b = SLABS[s - 1][1], SLABS[s - 1][4]
                    k = 4 * (2 - b) + n
                    dve.wait_ge(s_bhi, k + 1)
                    dve.tensor_tensor(bL[:, 2 * n:2 * n + 2, :].rearrange("p c t -> p (c t)"), BR[:, k % 2, :],
                                      bH[:, 2 * n:2 * n + 2, :].rearrange("p c t -> p (c t)"),
                                      ALU.subtract).then_inc(s_blo, 1)
                if s == LAST:
                    for n in range(3):
                        merged_lo(n)

            def merged_lo(n):
                dve.wait_ge(s_mhi, n + 1)
                dve.scalar_tensor_tensor(out=hL[:, 2 * n:2 * n + 2, :].rearrange("p c t -> p (c t)"),
                                         in0=M[:, 2 * n:2 * n + 2, :].rearrange("p c t -> p (c t)"), scalar=0.5,
                                         in1=hH[:, 2 * n:2 * n + 2, :].rearrange("p c t -> p (c t)"),
                                         op0=ALU.mult, op1=ALU.subtract).then_inc(s_mlo, 1)

            def early(s):
                u = s - U0
                if 0 <= u < NU:
                    dve.wait_ge(s_hp, u + 1)
                    if u >= 2:
                        dve.wait_ge(s_hpv, u - 1)
                    b0 = 2 + 2 * (u % 2)
                    n = P * (1 + u % 2)
                    link(dve.tensor_tensor(PM[:, u % 2, 0:n], ps[:, b0 + 1, 0:n], K[:, K_ID:K_ID + n], ALU.mult))
                    for lv in range(1, 8):
                        b = LEVELS[lv]
                        r = slice(0, b if lv == 1 else P)
                        to = PM[r, u % 2, 0:P].rearrange("p (n w) -> p n w", w=2 * b)[:, :, b:2 * b]
                        c = slice(64 * (lv - 1), 64 * lv)
                        last = dve.copy_predicated(to, K[r, c].bitcast(mybir.dt.uint32).rearrange(
                            "p (n w) -> p n w", w=b), ps[r, b0, c].rearrange("p (n w) -> p n w", w=b))
                        if lv < 7:
                            link(last)
                    last.then_inc(s_hmask, 1)
                h = s - H0 - 2
                if 0 <= h < HEADS:
                    dve.wait_ge(s_at, h + 1)
                    if h >= 2:
                        dve.wait_ge(s_apv, h // 2)
                    dve.tensor_copy(PTS[h % 2][:, 512:768], ps[:, 5, 0:256]).then_inc(s_apv2, 1)
                h = s - H0
                if 0 <= h < HEADS:
                    dve.wait_ge(s_as, h + 1)
                    dve.tensor_reduce(st_t4[:, 0:2], ps[:, 2, :].rearrange("p (a k) -> p a k", a=2), AX_X, ALU.max)
                    link(dve.tensor_reduce(st_t4[:, 2:4], ps[:, 3, 0:256].rearrange("p (a k) -> p a k", a=2),
                                           AX_X, ALU.max))
                    dve.tensor_scalar(st_nb[:, h % 2], st_t4, -SCALE, None, ALU.mult).then_inc(s_nb, 1)
                if s == SC + 1:
                    dve.wait_ge(s_cpe, 4)
                    for i in range(TT):
                        sc = ps[:, 7 - i, :].rearrange("p (h b c) -> p b h c", b=2, c=16)
                        cm = K[:, K_CMASK + 15 * i:K_CMASK + 15 * i + 15].rearrange("p (a c) -> p a c", a=1)
                        last = dve.scalar_tensor_tensor(out=SM[:, i], in0=sc[:, 0, :, 0:NCMP], scalar=SCALE,
                                                        in1=cm.to_broadcast((P, HEADS, NCMP)),
                                                        op0=ALU.mult, op1=ALU.add)
                    link(last)
                    for i in range(TT):
                        sc = ps[:, 7 - i, :].rearrange("p (h b c) -> p b h c", b=2, c=16)
                        last = dve.scalar_tensor_tensor(out=SM[:, i], in0=sc[:, 1, :, 0:NCMP], scalar=SCALE,
                                                        in1=SM[:, i], op0=ALU.mult, op1=ALU.add)
                    link(last)
                    smf = SM.rearrange("p i h c -> p (i h) c")
                    link(dve.tensor_reduce(st_mx, smf, AX_X, ALU.max))
                    mxv = st_mx.rearrange("p (h c) -> p h c", c=1)
                    dve.tensor_tensor(smf, smf, mxv.to_broadcast((P, 32, NCMP)), ALU.subtract).then_inc(s_csm, 1)
                if s == SC + 2:
                    dve.wait_ge(s_cexp, 1)
                    dve.wait_ge(s_gg, 1)
                    smf = SM.rearrange("p i h c -> p (i h) c")
                    link(dve.tensor_reduce(st_cs, smf, AX_X, ALU.add))
                    link(dve.tensor_scalar(st_cs, st_cs, 1e-30, None, ALU.max))
                    link(dve.reciprocal(st_cs, st_cs))
                    for i in range(TT):
                        gv = GT[:, i, :].rearrange("p (h j) -> p h j", j=3)[:, :, 0]
                        last = dve.scalar_tensor_tensor(out=st_mx[:, 16 * i:16 * i + 16],
                                                        in0=st_cs[:, 16 * i:16 * i + 16],
                                                        scalar=K[:, K_VALID + i:K_VALID + i + 1], in1=gv,
                                                        op0=ALU.mult, op1=ALU.mult)
                    link(last)
                    mxv = st_mx.rearrange("p (h c) -> p h c", c=1)
                    dve.tensor_tensor(PC.rearrange("p i h c -> p (i h) c")[:, :, 0:NCMP], smf,
                                      mxv.to_broadcast((P, 32, NCMP)), ALU.mult).then_inc(s_cpc, 1)

            def late(s):
                h = s - H0
                if 0 <= h < HEADS:
                    dve.wait_ge(s_exp, h + 1)
                    if h >= 2:
                        dve.wait_ge(s_scl, h - 1)
                    w = st_w[:, h % 2]
                    link(dve.tensor_scalar(w, st_sum[:, h % 2], 1e-30, None, ALU.max))
                    link(dve.reciprocal(w, w))
                    dve.tensor_tensor(w[:, 0:2], w[:, 0:2], GT[:, 1, 3 * h + 1:3 * h + 3], ALU.mult)
                    dve.tensor_tensor(w[:, 2:4], w[:, 2:4], GT[:, 0, 3 * h + 1:3 * h + 3], ALU.mult)\
                        .then_inc(s_aw, 1)

            def read(s):
                kind, n = SLABS[s][:2]
                if kind not in BY_DVE:
                    return
                dve.wait_ge(s_prod, s + 1)
                if kind in ("q", "ks", "kw", "silu", "branch", "out"):
                    dve.wait_ge(s_read_a, ACT_READS[s if kind != "branch" else s - 1])
                b = bank(s)
                b2 = b.rearrange("p (c t) -> p c t", c=2)
                if kind == "hq":
                    last = dve.tensor_copy(HQ[:, 2 * n:2 * n + 2, :], b2)
                elif kind == "q":
                    for src, own, other in query_halves(s):
                        last = dve.tensor_tensor(other, src, own, ALU.subtract)
                elif kind == "hv":
                    last = dve.tensor_copy(HV[:, :, SLAB * n:SLAB * n + SLAB], b2)
                elif kind in ("kc", "vc"):
                    v = 0 if kind == "kc" else 1
                    pos = V[:, V_PEK + CB * v:V_PEK + CB * v + CB].rearrange("p (r j k) -> p r k j", r=2, k=2)
                    for r in range(2):
                        win = b2[:, :, CS * r:CS * r + CS * NCMP].rearrange("p q (c j k) -> p k j q c", j=CS // 2, k=2)
                        to = cpe[:, v, 8 * r:8 * r + 8].rearrange("p j (q e) c -> p e j q c", e=2)
                        for e in range(2):
                            h = slice(64 * e, 64 * e + 64)
                            for k in range(2):
                                pv = pos[h, r, k].rearrange("p (j q c) -> p j q c", q=1, c=1)
                                last = dve.tensor_tensor(to[64 * k:64 * k + 64, e], win[h, k],
                                                         pv.to_broadcast((64, CS // 2, 2, NCMP)), ALU.add)
                elif kind in ("ks", "kw"):
                    for (src, own, other), (_, hi_own, _) in zip(key_halves(s, 1), key_halves(s, 0)):
                        dve.tensor_tensor(own, src, hi_own, ALU.subtract)
                        last = dve.tensor_tensor(other, src, hi_own, ALU.subtract)
                elif kind in ("vs", "vw"):
                    last = dve.tensor_copy(VV[:, 0 if kind == "vs" else 1], b2)
                elif kind == "silu":
                    br = SLABS[s][4]
                    k = 4 * (2 - br) + n
                    if br < 2 and n == 0:
                        dve.wait_ge(s_madd, 4 * (2 - br))
                    dve.scalar_tensor_tensor(out=U, in0=TG[:, tslot(s), :], scalar=1.0, in1=b, op0=ALU.add,
                                             op1=ALU.mult).then_inc(s_read_v, 1)
                    dve.wait_ge(s_read_v, DVE_READS[s])
                    src = (OA, MX, OC)[br][:, 2 * n:2 * n + 2, :].rearrange("p c t -> p (c t)")
                    if br == 0:
                        dve.wait_ge(s_aoa, HG)
                    if br == 1:
                        dve.wait_ge(s_px, 4)
                    if k >= 2:
                        dve.wait_ge(s_bhi, k - 1)
                    dve.tensor_tensor(BR[:, k % 2, :], src, U, ALU.mult).then_inc(s_br, 1)
                    return
                elif kind == "branch":
                    br = SLABS[s][4]
                    k = 4 * (2 - br) + n
                    if k:
                        dve.wait_ge(s_madd, min(k, 8))
                    if k > 8:
                        dve.wait_ge(s_mfin, k - 8)
                    dve.scalar_tensor_tensor(out=U, in0=TG[:, tslot(s - 1), :], scalar=1.0, in1=b, op0=ALU.add,
                                             op1=ALU.mult).then_inc(s_read_v, 1)
                    if br == 0:
                        dve.wait_ge(s_read_v, DVE_READS[s])
                        m = M[:, 2 * n:2 * n + 2, :].rearrange("p c t -> p (c t)")
                        dve.tensor_tensor(m, m, U, ALU.add).then_inc(s_mfin, 1)
                    return
                elif kind == "out":
                    dve.wait_ge(s_post, 16)
                    pv = POST[:, SLAB * n:SLAB * n + SLAB].rearrange("p (a n) -> p a n", a=1)
                    last = dve.tensor_tensor(Y[:, :, SLAB * n:SLAB * n + SLAB], b2,
                                             pv.to_broadcast((P, TT, SLAB)), ALU.mult)
                last.then_inc(s_read_v, 1)

            dve.memset(st_eps, EPS).then_inc(s_init, 1)
            dve.memset(CKS[:, :, :, NCMP:16].bitcast(F32), 0.0)
            for i, n in ((0, D), (1, D // 2), (1, D)):
                if n == D // 2 or i == 0:
                    dve.wait_ge(s_hx, i + 1)
                    link(dve.reciprocal(st_r[:, i:i + 1], st_t[:, i:i + 1]))
                part = xin[:, i, (D // 2 if i and n == D else 0):n]
                dve.tensor_scalar(part, part, st_r[:, i:i + 1], None, ALU.mult).then_inc(s_xn, 1)

            dve.wait_ge(s_hi0a, 1)
            dve.tensor_tensor(WL[:, 0, 0:FIRST_A, :], W[:, 0, 0:FIRST_A, :], WH[:, 0, 0:FIRST_A, :],
                              ALU.subtract).then_inc(s_lo0, 1)
            dve.wait_ge(s_land[0], 16)
            dve.tensor_copy(WH[:, 0, FIRST_A:KC, :], W[:, 0, FIRST_A:KC, :]).then_inc(s_hi0b, 1)
            dve.wait_ge(s_small, 32)
            for c in range(KC):
                dve.wait_ge(s_hx, TT + 2 * (c // 2) + 2)
                dve.scalar_tensor_tensor(out=hL[:, c, :], in0=ps[:, 2 + c // 2, 256 * (c % 2):256 * (c % 2) + 256],
                                         scalar=V[:, V_PRE + c:V_PRE + c + 1], in1=hH[:, c, :],
                                         op0=ALU.mult, op1=ALU.subtract).then_inc(s_lx, 1)
            dve.wait_ge(s_hi0b, 1)
            dve.tensor_tensor(WL[:, 0, FIRST_A:FIRST_B, :], W[:, 0, FIRST_A:FIRST_B, :], WH[:, 0, FIRST_A:FIRST_B, :],
                              ALU.subtract).then_inc(s_lo, 1)
            dve.tensor_tensor(st_lb[:, 0], V[:, V_LB:V_LB + 8], V[:, V_LB:V_LB + 8], ALU.subtract).then_inc(s_lbd, 1)
            lo(1)
            dve.wait_ge(s_lbe, 1)
            link(dve.reciprocal(st_lb[:, 2], st_lb[:, 1]))
            link(dve.tensor_tensor(st_lb[:, 2], st_lb[:, 2], st_lb[:, 1], ALU.mult))
            link(dve.tensor_tensor(st_lb[:, 3], st_lb[:, 2], st_lb[:, 2], ALU.subtract))
            link(dve.tensor_scalar(st_lb[:, 4], st_lb[:, 3], -1.0, 1.0, ALU.mult, ALU.add))
            dve.tensor_copy(IB[:], ident)
            dve.tensor_copy(st_hn, V[:, V_HN:V_HN + 8])
            link(dve.tensor_scalar(st_ps, V[:, V_PS:V_PS + 8], 0.5, None, ALU.mult))
            link(dve.tensor_scalar(st_hn, st_hn, 0.5, None, ALU.mult))
            dve.wait_ge(s_consts, 48)
            dve.tensor_copy(MB[:], causal)
            for s in range(NS - 1):
                early(s)
                if mixing(s - 1):
                    lo(s + 1)
                mix(s)
                read(s)
                if s == LAST:
                    merged_lo(3)
                if s + 2 < NS and not mixing(s):
                    lo(s + 2)
                late(s)
            dve.wait_ge(s_xr, 16)
            n = slice(SLAB * 3, D)
            for i in range(TT):
                dve.wait_ge(s_osq, i + 1)
                dve.tensor_reduce(st_t[:, i:i + 1], st_o[:, i:i + 1, :], AX_X, ALU.add).then_inc(s_fin_ss, 1)
                link(dve.tensor_tensor(Y[:, i, n], last_rows(i), POST[:, n], ALU.mult))
                dve.wait_ge(s_root, i + 1)
                link(dve.reciprocal(st_r[:, i:i + 1], st_q[:, i:i + 1]))
                for half in range(2):
                    c = slice(D // 2 * half, D // 2 * half + D // 2)
                    dve.scalar_tensor_tensor(out=OUT[:, i, c], in0=Y[:, i, c], scalar=st_r[:, i:i + 1],
                                             in1=XR[:, i, c], op0=ALU.mult, op1=ALU.add).then_inc(s_fin, 1)

        @block.tensor
        def _(pe):
            def compressed_scores(i, h):
                o = ps[:, 7 - i, 32 * h:32 * h + 32].rearrange("p (b c) -> p b c", b=2)
                return pe.matmul(o, queries(h, i), CKS[:, :, h // HPG, :], start=(h == 0), stop=(h == HEADS - 1))

            def product(s):
                kind, n = SLABS[s][:2]
                pe.wait_ge(s_lo, s + 1)
                small = []
                if s == SC:
                    pe.wait_ge(s_ck, 1)
                    pe.wait_ge(s_cvd, 1)
                    pe.wait_ge(s_read_v, DVE_READS[WHERE[("q", 3)]])
                    small = [(i, h) for i in range(TT) for h in range(HEADS)]
                if s >= 2:
                    if SLABS[s - 2][0] in BY_ACT:
                        pe.wait_ge(s_read_a, ACT_READS[s - 2])
                    if SLABS[s - 2][0] in BY_DVE:
                        pe.wait_ge(s_read_v, DVE_READS[s - 2])
                ah, al = (bH, bL) if kind == "branch" else (hH, hL)
                wh, wl = WH[:, s % 3], WL[:, s % 2]
                w = width(s)
                split = kind == "out" and n == 0
                order = [(c, k) for c in range(1 if kind == "gate" else 2) for k in range(KC)]
                if split:
                    order.sort(key=lambda ck: ck[1])
                for c, k in order:
                    if kind == "branch" and n == 0 and c == 0 and k % 2 == 0:
                        pe.wait_ge(s_blo, 4 * (2 - SLABS[s][4]) + k // 2 + 1)
                    if kind == "out" and n == 0 and c == 0 and k % 2 == 0:
                        pe.wait_ge(s_mlo, k // 2 + 1)
                    if kind in TOKEN_MAJOR:
                        o = last_rows(c) if s == NS - 1 else bank(s)[:, w * c:w * c + w]
                        pairs = [(a[:, k, P * c:P * c + P], b[:, k, 0:w])
                                 for a, b in ((ah, wl), (al, wh), (ah, wh))]
                    else:
                        o = bank(s)[:, T * c:T * c + T]
                        m = min(w, P)
                        if kind == "gate":
                            o = bank(s)[0:GATES, 0:T]
                        pairs = [(b[:, k, P * c:P * c + m], a[:, k, :])
                                 for a, b in ((ah, wl), (al, wh), (ah, wh))]
                    for j, (l, r) in enumerate(pairs):
                        mm = pe.matmul(o, l, r, start=(k == 0 and j == 0 and not (split and c)),
                                       stop=(k == KC - 1 and j == 2 and not (split and not c)))
                        if small:
                            i, h = small.pop(0)
                            last = compressed_scores(i, h)
                            if not small:
                                last.then_inc(s_cpe, 1)
                    if s == NS - 1 and k == KC - 1:
                        mm.then_inc(s_last, 1)
                if s < NS - 1:
                    mm.then_inc(s_prod, 1)

            def hg_scores(u):
                h, i = u // 2, u % 2
                p, hp = h // 2, h % 2
                if i == 0:
                    pe.wait_ge(s_hmul, h + 1)
                if u >= 2:
                    pe.wait_ge(s_hmask, u - 1)
                b0 = 2 + 2 * (u % 2)
                q = QK[p % 2]
                for lv in range(1, 8):
                    b = LEVELS[lv]
                    t = q[:, lv, hp, P * i:P * i + P]
                    up = t.rearrange("p (n w) -> p n w", w=2 * b)[:, :, b:2 * b]
                    if lv == 1:
                        pe.matmul(ps[0:b, b0, 0:64], t[:, 0:b], up, start=True, stop=True)
                    else:
                        pe.matmul(ps[:, b0, 64 * (lv - 1):64 * lv], t, up, start=(lv == 2), stop=(lv == 7))
                mm = pe.matmul(ps[:, b0 + 1, 0:P], ones, HQ[:, h, P * i:P * i + P], start=True, stop=(i == 0))
                if i:
                    mm = pe.matmul(ps[:, b0 + 1, P:2 * P], q[:, 0, hp, 0:P], q[:, 0, hp, P:T], start=False, stop=True)
                mm.then_inc(s_hp, 1)

            def hg_values(u):
                h, i = u // 2, u % 2
                pe.wait_ge(s_hmask, u + 1)
                pe.wait_ge(s_read_v, DVE_READS[WHERE[("hv", h // 2)]])
                if h and i == 0:
                    pe.wait_ge(s_hoc, h)
                o = ps[:, 6, P * i:P * i + P]
                v = HV[:, i, P * h:P * h + P]
                pm = PM[:, u % 2]
                mm = pe.matmul(o, v, pm[:, 0:P], start=True, stop=(i == 0))
                if i:
                    mm = pe.matmul(o, HV[:, 0, P * h:P * h + P], pm[:, P:2 * P], start=False, stop=True)
                mm.then_inc(s_hpv, 1)

            def compress(a):
                pe.wait_ge(s_cw, 32)
                pe.wait_ge(s_read_v, DVE_READS[WHERE[("vc", 0)]])
                if a:
                    pe.wait_ge(s_hoc, HG)
                for j in range(CB // 2):
                    rows = cpe[:, a, j].rearrange("p g c -> p (g c)")
                    if a:
                        mm = pe.matmul(ps[0:GROUPS * NCMP, 6, 0:HEAD], rows, WC[:, a, j, :],
                                       start=(j == 0), stop=(j == CB // 2 - 1))
                    else:
                        mm = pe.matmul(ps[0:HEAD, 5, 0:GROUPS * NCMP], WC[:, a, j, :], rows,
                                       start=(j == 0), stop=(j == CB // 2 - 1))
                mm.then_inc(s_cpe, 1)

            def mix(s):
                if 0 <= s - U0 < NU:
                    hg_scores(s - U0)
                if 0 <= s - U0 - 1 < NU:
                    hg_values(s - U0 - 1)
                for p in range(HG // 2):
                    if s == U0 + 5 + 4 * p:
                        pe.wait_ge(s_hsq, 2 * p + 2)
                        if p:
                            pe.wait_ge(s_hrs, p)
                        pe.matmul(ps[:, 7, :], ones, SQ.rearrange("p e t -> p (e t)"), start=True,
                                  stop=True).then_inc(s_hss, 1)
                if s == CK:
                    pe.wait_ge(s_read_a, ACT_READS[WHERE[("gate", 0)]])
                    for i in range(TT):
                        mm = pe.transpose(ps[:, 4, GATES * i:GATES * i + GATES], GL[0:GATES, P * i:P * i + P],
                                          ident[0:GATES, 0:GATES])
                    mm.then_inc(s_gt, 1)
                    compress(0)
                if s == CV:
                    compress(1)
                if s == CX:
                    pe.wait_ge(s_cv, 1)
                    pe.wait_ge(s_sel, 16)
                    for g in range(GROUPS):
                        mm = pe.matmul(ps[:, 6, HEAD * g:HEAD * g + HEAD], SEL[0:GROUPS * NCMP, P * g:P * g + P],
                                       CSB, start=(g == 0), stop=(g == GROUPS - 1))
                    mm.then_inc(s_cpe, 1)
                if s == TURN:
                    pe.wait_ge(s_cpc, 1)
                    pe.wait_ge(s_cvd, 1)
                    for g in range(GROUPS):
                        for i in range(TT):
                            mm = pe.transpose(ps[:, 6 + g // 2, 256 * (g % 2) + P * i:256 * (g % 2) + P * i + P],
                                              PC[:, i, 4 * g:4 * g + 4, :].rearrange("p h c -> p (h c)"), ident)
                    mm.then_inc(s_cpe, 1)
                if 0 <= s - H0 - 3 < HEADS and (s - H0 - 3) % 2:
                    at_values((s - H0 - 3) // 2)
                if 0 <= s - H0 - 2 < HEADS:
                    at_turn(s - H0 - 2)
                if 0 <= s - H0 < HEADS:
                    at_scores(s - H0)
                g = s - G0
                if 0 <= g < 4:
                    pe.wait_ge(s_pool, g + 1)
                    pe.wait_ge(s_pw, 64)
                    if g == 0:
                        pe.wait_ge(s_pct, 1)
                    else:
                        pe.wait_ge(s_px, g)
                    for c in range(2):
                        for k in range(2):
                            mm = pe.matmul(ps[:, 7, 256 * c:256 * c + 256], PW[:, g, k, P * c:P * c + P],
                                           BV[:, 2 * g + k, :], start=(k == 0), stop=(k == 1))
                    mm.then_inc(s_pmix, 1)

            def at_scores(h):
                g = h // HPG
                if h == 0:
                    pe.wait_ge(s_read_v, DVE_READS[WHERE[("kw", 0)]])
                else:
                    pe.wait_ge(s_exp, h)
                mask = MB[:].rearrange("p (a k) -> p a k", a=1).to_broadcast((P, 2, P))
                for part in range(2):
                    pe.matmul(ps[:, 2, :], queries(h, 1), KS[:, part, g].rearrange("p a t -> p (a t)"),
                              start=(part == 0), stop=False)
                pe.matmul(ps[:, 2, :].rearrange("p (a k) -> p a k", a=2)[:, :, P:T], IB[:], mask,
                          start=False, stop=True)
                for part in range(2):
                    pe.matmul(ps[:, 3, 0:256].rearrange("p (a k) -> p a k", a=2), queries(h, 0),
                              KS[:, part, g, :, 0:P], start=(part == 0), stop=False)
                pe.matmul(ps[:, 3, 0:256].rearrange("p (a k) -> p a k", a=2), IB[:], mask,
                          start=False, stop=True).then_inc(s_as, 1)

            def at_turn(h):
                pe.wait_ge(s_scl, h + 1)
                if h:
                    pe.wait_ge(s_apt, h)
                    pe.wait_ge(s_apv2, h)
                pp = PP[:, h % 2]
                o = ps_flat[:, 512 * 4:512 * 4 + 768]
                for a in range(2):
                    pe.transpose(o[:, 384 * a:384 * a + 128], pp[:, 512 + 128 * a:640 + 128 * a], ident)
                    pe.transpose(o[:, 384 * a + 128:384 * a + 256], pp[:, 256 * a:256 * a + 128], ident)
                    mm = pe.transpose(o[:, 384 * a + 256:384 * a + 384], pp[:, 256 * a + 128:256 * a + 256], ident)
                mm.then_inc(s_at, 1)

            def at_values(pair):
                pe.wait_ge(s_apt, 2 * pair + 2)
                pe.wait_ge(s_apv2, 2 * pair + 2)
                if pair == 0:
                    pe.wait_ge(s_pct, 1)
                    pe.wait_ge(s_pct_a, 1)
                else:
                    pe.wait_ge(s_aoa, pair)

                def steps(h):
                    g = h // HPG
                    d = slice(HEAD * g, HEAD * g + HEAD)
                    pt = PTS[h % 2]
                    out = [(0, CVD[:, h % HPG, d], PCT[:, g, :])]
                    for a in range(2):
                        out += [(0, VV[:, a, 0, d], pt[:, 384 * a:384 * a + 256]),
                                (P, VV[:, a, 1, d], pt[:, 384 * a + 256:384 * a + 384])]
                    return out

                both = [steps(2 * pair), steps(2 * pair + 1)]
                count = len(both[0])
                for j in range(count):
                    for hh in range(2):
                        at, v, p = both[hh][j]
                        mm = pe.matmul(ps[64 * hh:64 * hh + 64, 6, at:T], v, p, start=(j == 0), stop=(j == count - 1))
                mm.then_inc(s_apv, 1)

            def first_product():
                steps = [(WH, hH, k) for k in range(KC)] + [(WH, hL, k) for k in range(KC)] \
                    + [(WL, hH, k) for k in range(KC)]
                for j, (w, h, k) in enumerate(steps):
                    if j < KC:
                        pe.wait_ge(s_hx, TT + k + 1)
                        pe.wait_ge(s_hi0a if k < FIRST_A else s_hi0b, 1)
                    elif j < 2 * KC:
                        pe.wait_ge(s_lx, k + 1)
                    else:
                        pe.wait_ge(s_lo0 if k < FIRST_A else s_lo if k < FIRST_B else s_lo0p, 1)
                    for c in range(2):
                        mm = pe.matmul(bank(0)[:, T * c:T * c + T], w[:, 0, k, P * c:P * c + P], h[:, k, :],
                                       start=(j == 0 and c == 0), stop=(j == len(steps) - 1 and c == 1))
                mm.then_inc(s_prod, 1)

            pe.wait_ge(s_small, 32)
            for i in range(TT):
                for c in range(KC):
                    pe.wait_ge(s_xn, 1 + (2 if c >= KC // 2 else 1) * i)
                    mm = pe.transpose(ps[:, 2 + c // 2, 256 * (c % 2) + P * i:256 * (c % 2) + P * i + P],
                                      xin[:, i, P * c:P * c + P], ident)
                    if i and c % 2:
                        mm.then_inc(s_xt, 1)
            first_product()
            for s in range(1, NS):
                mix(s)
                product(s)


def mixing(s):
    return U0 <= s < U0 + NU or H0 <= s < H0 + HEADS


def tslot(s):
    return s % 2


def constant_table():
    import numpy as np
    k = np.zeros((P, K_COLS), np.float32)
    s = np.arange(P)[:, None]
    j = np.arange(64)[None, :]
    for n, b in enumerate(LEVELS[1:]):
        t = (j // b) * 2 * b + b + j % b
        k[:, K_MASK + 64 * n:K_MASK + 64 * n + 64] = (s // (2 * b) == t // (2 * b)) & (s % (2 * b) < b)
    k[:, K_ID:K_ID + P] = np.eye(P)
    k[:, K_ONE:K_ONE + P] = 1.0
    k[:, K_CAUSAL:K_CAUSAL + P] = np.where(np.arange(P)[None, :] <= s, 0.0, -1e30)
    for i in range(TT):
        t = i * P + s
        end = np.arange(NCMP)[None, :] * CS + CB - 1
        k[:, K_CMASK + 15 * i:K_CMASK + 15 * i + 15] = np.where(end <= t, 0.0, -1e30)
        k[:, K_VALID + i] = (t[:, 0] >= CB - 1)
    for g, w in enumerate(WINDOWS):
        k[:, K_COUNT + 16 * g:K_COUNT + 16 * g + 16] = 1.0 / np.minimum(np.arange(16) + 1, w)
    for i in range(4):
        k[32 * i:32 * i + 32, K_ROWS + i] = 1.0
        for g in range(GROUPS):
            for c in range(NCMP):
                k[NCMP * g + c, K_SEL + P * g + 32 * i + c] = 1.0
    return k


def kernel(x, pre_norm, w_in, cmp_pe_k, cmp_pe_v, cmp_w_k, cmp_w_v, pool_w, pool_scale,
           hgrn_lb_logits, hgrn_norm, w_branch, w_out, post_norm):
    import numpy as np
    import concourse.bacc as bacc
    from concourse.bass_utils import run_bass_kernel_spmd

    def by_partition(v):
        return np.asarray(v).reshape(KC, P).T

    def twice(pe):
        t = np.asarray(pe)[0].T
        return np.concatenate([t, t], axis=0)

    small = np.ascontiguousarray(np.concatenate(
        [by_partition(pre_norm), by_partition(hgrn_lb_logits), by_partition(hgrn_norm), by_partition(pool_scale),
         twice(cmp_pe_k), twice(cmp_pe_v)], axis=1))
    arrays = {
        "x": np.ascontiguousarray(x), "small": small, "consts": constant_table(),
        "w_in": np.ascontiguousarray(w_in),
        "cmp_w": np.ascontiguousarray(np.concatenate([np.asarray(cmp_w_k), np.asarray(cmp_w_v)], axis=0)),
        "pool_w": np.ascontiguousarray(pool_w), "w_branch": np.ascontiguousarray(w_branch),
        "w_out": np.ascontiguousarray(w_out), "post_norm": np.ascontiguousarray(post_norm),
    }
    nc = bacc.Bacc("TRN2", target_bir_lowering=False, num_devices=1)
    args = [nc.dram_tensor(n, a.shape, mybir.dt.from_np(a.dtype), kind="ExternalInput").ap()
            for n, a in arrays.items()]
    out = nc.dram_tensor("out", (1, T, D), F32, kind="ExternalOutput").ap()
    trunk(nc, *args, out)
    r = run_bass_kernel_spmd(nc, [arrays], core_ids=[0])
    return r.results[0]["out"]
```
